# Optimizing a Trainium2 kernel written in Bass

```python
import math
import jax
import jax.numpy as jnp
from jax import lax
import numpy as np

D_MODEL = 2048
BATCH = 1
SEQ = 512
DEPTH = 1

HEAD_DIM = 128
ATTN_GROUPS = ((128, 1), (512, 4), (2048, 16))
ATTN_HEADS_PER_GROUP = D_MODEL // 512
ATTN_HEADS = ATTN_HEADS_PER_GROUP * len(ATTN_GROUPS)
ATTN_WIDTH = ATTN_HEADS * HEAD_DIM
ATTN_OUT_WIDTH = ATTN_HEADS_PER_GROUP * HEAD_DIM
ATTN_BLOCK = 128
ROPE_THETA = 500000.0
ROPE_DIM = HEAD_DIM // 4
DN_HEADS = D_MODEL // 128
DN_KEY_DIM = 128
DN_VAL_DIM = 128
DN_QK_WIDTH = DN_HEADS * DN_KEY_DIM
DN_V_WIDTH = DN_HEADS * DN_VAL_DIM
DN_CONV_WIDTH = 4
DN_CHUNK = 64
PEER_HEADS = 8
PEER_KEYS = 128
PEER_EXPERTS = PEER_KEYS * PEER_KEYS
PEER_QUERY_DIM = 128
PEER_TOPK = 16
PEER_TOKEN_BLOCK = 128
NORM_EPS = 1e-6
IN_SPLIT_SIZES = (3 * ATTN_WIDTH, 2 * DN_QK_WIDTH + DN_V_WIDTH, DN_V_WIDTH, DN_HEADS, DN_HEADS, 2 * D_MODEL)
IN_WIDTH = sum(IN_SPLIT_SIZES)

kernel_name = 'hybrid_dilated_attn_deltanet_peer_block'

def rmsnorm(x, w):
    xf = x.astype(jnp.float32)
    y = xf * lax.rsqrt(jnp.mean(xf * xf, axis=-1, keepdims=True) + NORM_EPS)
    return (y * w.astype(jnp.float32)).astype(x.dtype)

def l2norm(t):
    return t * lax.rsqrt(jnp.sum(t * t, axis=-1, keepdims=True) + 1e-6)

def partial_rotary(t, positions):
    half = ROPE_DIM // 2
    inv_freq = ROPE_THETA ** (-jnp.arange(half, dtype=jnp.float32) * (2.0 / ROPE_DIM))
    ang = positions.astype(jnp.float32)[:, None] * inv_freq[None, :]
    cos = jnp.cos(ang)[None, :, None, :]
    sin = jnp.sin(ang)[None, :, None, :]
    tf = t.astype(jnp.float32)
    t1, t2 = tf[..., :half], tf[..., half:ROPE_DIM]
    out = jnp.concatenate([t1 * cos - t2 * sin, t2 * cos + t1 * sin, tf[..., ROPE_DIM:]], axis=-1)
    return out.astype(t.dtype)

def dilated_window_attention(q, k, v, window, dilation):
    B, S, H, hd = q.shape
    n_back = window // dilation
    L = S // dilation
    nb = -(-L // ATTN_BLOCK)
    Lp = nb * ATTN_BLOCK

    def to_blocks(t):
        t = t.reshape(B, L, dilation, H, hd).transpose(0, 2, 1, 3, 4)
        t = jnp.pad(t, ((0, 0), (0, 0), (0, Lp - L), (0, 0), (0, 0)))
        return t.reshape(B, dilation, nb, ATTN_BLOCK, H, hd)

    def band(t):
        prev = jnp.pad(t, ((0, 0), (0, 0), (1, 0), (0, 0), (0, 0), (0, 0)))[:, :, :-1]
        return jnp.concatenate([prev, t], axis=3)

    qb = to_blocks(q).astype(jnp.float32)
    kk = band(to_blocks(k)).astype(jnp.float32)
    vv = band(to_blocks(v)).astype(jnp.float32)
    s = jnp.einsum('brnqhd,brnkhd->brnhqk', qb, kk) * (hd ** -0.5)
    qi = jnp.arange(ATTN_BLOCK)[:, None]
    kj = jnp.arange(2 * ATTN_BLOCK)[None, :]
    dist = qi + ATTN_BLOCK - kj
    valid = (dist >= 0) & (dist <= n_back)
    not_before_start = (jnp.arange(nb)[:, None, None] > 0) | (kj[None] >= ATTN_BLOCK)
    mask = valid[None] & not_before_start
    s = jnp.where(mask[None, None, :, None], s, -jnp.inf)
    lse = jax.nn.logsumexp(s, axis=-1)
    p = jnp.exp(s - lse[..., None])
    o = jnp.einsum('brnhqk,brnkhd->brnqhd', p, vv)
    o = o.reshape(B, dilation, Lp, H, hd)[:, :, :L].transpose(0, 2, 1, 3, 4).reshape(B, S, H, hd)
    lse = lse.transpose(0, 1, 2, 4, 3).reshape(B, dilation, Lp, H)[:, :, :L]
    lse = lse.transpose(0, 2, 1, 3).reshape(B, S, H)
    return o, lse

def short_conv(x, w):
    C = x.shape[-1]
    return lax.conv_general_dilated(
        x, w.astype(x.dtype)[:, None, :], window_strides=(1,),
        padding=((DN_CONV_WIDTH - 1, 0),), dimension_numbers=('NWC', 'WIO', 'NWC'),
        feature_group_count=C)

def gated_delta_rule(q, k, v, g, beta):
    B, S, H, dk = q.shape
    dv = v.shape[-1]
    C = DN_CHUNK
    nc = S // C

    def chunks(t):
        return t.reshape(B, nc, C, H, -1).transpose(1, 0, 3, 2, 4)

    qc, kc, vc = chunks(q), chunks(k), chunks(v)
    gc = g.reshape(B, nc, C, H).transpose(1, 0, 3, 2)
    bc = beta.reshape(B, nc, C, H).transpose(1, 0, 3, 2)
    gam = jnp.cumsum(gc, axis=-1)
    i = jnp.arange(C)[:, None]
    j = jnp.arange(C)[None, :]
    diff = gam[..., :, None] - gam[..., None, :]
    decay = jnp.where(i >= j, jnp.exp(jnp.where(i >= j, diff, 0.0)), 0.0)
    kb = kc * bc[..., None]
    lmat = jnp.where(i > j, jnp.einsum('nbhid,nbhjd->nbhij', kb, kc) * decay, 0.0)
    rhs = jnp.concatenate([vc * bc[..., None], kb * jnp.exp(gam)[..., None]], axis=-1)
    sol = lax.linalg.triangular_solve(lmat, rhs, left_side=True, lower=True, unit_diagonal=True)
    u, w = sol[..., :dv], sol[..., dv:]
    qk = jnp.einsum('nbhid,nbhjd->nbhij', qc, kc) * decay
    q_dec = qc * jnp.exp(gam)[..., None]
    k_dec = kc * jnp.exp(gam[..., -1:] - gam)[..., None]
    chunk_decay = jnp.exp(gam[..., -1])

    def step(state, inp):
        u_c, w_c, qk_c, qd_c, kd_c, cd_c = inp
        v_new = u_c - jnp.einsum('bhck,bhkv->bhcv', w_c, state)
        o = jnp.einsum('bhck,bhkv->bhcv', qd_c, state) + jnp.einsum('bhij,bhjv->bhiv', qk_c, v_new)
        state = state * cd_c[..., None, None] + jnp.einsum('bhck,bhcv->bhkv', kd_c, v_new)
        return state, o

    state0 = jnp.zeros((B, H, dk, dv), jnp.float32)
    _, o = lax.scan(step, state0, (u, w, qk, q_dec, k_dec, chunk_decay))
    return o.transpose(1, 0, 3, 2, 4).reshape(B, S, H, dv)

def token_mixer(h, w_in, conv_w, a_log, dt_bias, dn_norm_w, w_attn_out, w_delta_out, w_mix_out):
    B, S, _ = h.shape
    proj = h @ w_in
    split_points = [int(p) for p in np.cumsum(IN_SPLIT_SIZES)[:-1]]
    attn_qkv, dn_qkv, dn_z, dn_b, dn_a, gates = jnp.split(proj, split_points, axis=-1)

    attn_qkv = attn_qkv.reshape(B, S, 3, ATTN_HEADS, HEAD_DIM)
    positions = jnp.arange(S)
    qa = partial_rotary(attn_qkv[:, :, 0], positions)
    ka = partial_rotary(attn_qkv[:, :, 1], positions)
    va = attn_qkv[:, :, 2]
    outs, lses = [], []
    for gi, (window, dilation) in enumerate(ATTN_GROUPS):
        hs = slice(gi * ATTN_HEADS_PER_GROUP, (gi + 1) * ATTN_HEADS_PER_GROUP)
        o, lse = dilated_window_attention(qa[:, :, hs], ka[:, :, hs], va[:, :, hs], window, dilation)
        outs.append(o)
        lses.append(lse)
    group_w = jax.nn.softmax(jnp.stack(lses, axis=0), axis=0)
    y_attn = jnp.sum(group_w[..., None] * jnp.stack(outs, axis=0), axis=0)
    y_attn = y_attn.reshape(B, S, ATTN_OUT_WIDTH).astype(h.dtype) @ w_attn_out

    dn_qkv = jax.nn.silu(short_conv(dn_qkv, conv_w))
    dq, dk, dvv = jnp.split(dn_qkv, [DN_QK_WIDTH, 2 * DN_QK_WIDTH], axis=-1)
    dq = l2norm(dq.reshape(B, S, DN_HEADS, DN_KEY_DIM).astype(jnp.float32)) * (DN_KEY_DIM ** -0.5)
    dk = l2norm(dk.reshape(B, S, DN_HEADS, DN_KEY_DIM).astype(jnp.float32))
    dvv = dvv.reshape(B, S, DN_HEADS, DN_VAL_DIM).astype(jnp.float32)
    beta = jax.nn.sigmoid(dn_b.astype(jnp.float32))
    g = -jnp.exp(a_log.astype(jnp.float32)) * jax.nn.softplus(dn_a.astype(jnp.float32) + dt_bias.astype(jnp.float32))
    o = gated_delta_rule(dq, dk, dvv, g, beta)
    o = rmsnorm(o, dn_norm_w) * jax.nn.silu(dn_z.reshape(B, S, DN_HEADS, DN_VAL_DIM).astype(jnp.float32))
    y_delta = o.reshape(B, S, DN_V_WIDTH).astype(h.dtype) @ w_delta_out

    gate_attn, gate_delta = jnp.split(jax.nn.sigmoid(gates), 2, axis=-1)
    merged = gate_attn * y_attn + gate_delta * y_delta
    return merged @ w_mix_out

def peer_ffn(h, w_query, sub_keys, expert_down, expert_up):
    B, S, D = h.shape
    T = B * S
    hb = h.reshape(T // PEER_TOKEN_BLOCK, PEER_TOKEN_BLOCK, D)

    def block(xb):
        tb = xb.shape[0]
        q = (xb @ w_query).reshape(tb, PEER_HEADS, 2, PEER_QUERY_DIM // 2).astype(jnp.float32)
        s = jnp.einsum('thpd,hpnd->thpn', q, sub_keys.astype(jnp.float32))
        half_s, half_i = lax.top_k(s, PEER_TOPK)
        cand_s = (half_s[:, :, 0, :, None] + half_s[:, :, 1, None, :]).reshape(tb, PEER_HEADS, PEER_TOPK * PEER_TOPK)
        cand_i = (half_i[:, :, 0, :, None] * PEER_KEYS + half_i[:, :, 1, None, :]).reshape(tb, PEER_HEADS, PEER_TOPK * PEER_TOPK)
        best_s, best_pos = lax.top_k(cand_s, PEER_TOPK)
        idx = jnp.take_along_axis(cand_i, best_pos, axis=-1)
        gw = jax.nn.softmax(best_s, axis=-1)
        u = jnp.take(expert_down, idx, axis=0)
        act = jax.nn.gelu(jnp.einsum('thkd,td->thk', u, xb).astype(jnp.float32), approximate=False)
        coef = (gw * act).astype(xb.dtype)
        vv = jnp.take(expert_up, idx, axis=0)
        return jnp.einsum('thk,thkd->td', coef, vv)

    out = lax.map(block, hb)
    return out.reshape(B, S, D)

def setup_inputs(seed: int = 0) -> dict:
    key = jax.random.key(seed)
    ks = jax.random.split(key, 20)
    f32 = jnp.float32

    def normal(k, shape, scale):
        return jax.random.normal(k, shape, f32) * scale

    def gain(k, shape):
        return 1.0 + normal(k, shape, 0.02)

    dt = jnp.exp(jax.random.uniform(ks[10], (DEPTH, DN_HEADS), f32, math.log(1e-3), math.log(1e-1)))
    return {
        'x': normal(ks[0], (BATCH, SEQ, D_MODEL), 1.0),
        'c': normal(ks[1], (BATCH, D_MODEL), 1.0),
        'w_ada': normal(ks[2], (DEPTH, D_MODEL, 6 * D_MODEL), 0.5 * D_MODEL ** -0.5),
        'b_ada': normal(ks[3], (DEPTH, 6 * D_MODEL), 0.02),
        'norm_pre_mix': gain(ks[4], (DEPTH, D_MODEL)),
        'norm_post_mix': gain(ks[5], (DEPTH, D_MODEL)),
        'norm_pre_ffn': gain(ks[6], (DEPTH, D_MODEL)),
        'norm_post_ffn': gain(ks[7], (DEPTH, D_MODEL)),
        'w_in': normal(ks[8], (DEPTH, D_MODEL, IN_WIDTH), D_MODEL ** -0.5),
        'conv_w': normal(ks[9], (DEPTH, DN_CONV_WIDTH, 2 * DN_QK_WIDTH + DN_V_WIDTH), DN_CONV_WIDTH ** -0.5),
        'a_log': jnp.log(jax.random.uniform(ks[11], (DEPTH, DN_HEADS), f32, 1.0, 16.0)),
        'dt_bias': dt + jnp.log(-jnp.expm1(-dt)),
        'dn_norm_w': gain(ks[12], (DEPTH, DN_VAL_DIM)),
        'w_attn_out': normal(ks[13], (DEPTH, ATTN_OUT_WIDTH, D_MODEL), ATTN_OUT_WIDTH ** -0.5),
        'w_delta_out': normal(ks[14], (DEPTH, DN_V_WIDTH, D_MODEL), DN_V_WIDTH ** -0.5),
        'w_mix_out': normal(ks[15], (DEPTH, D_MODEL, D_MODEL), D_MODEL ** -0.5),
        'peer_w_query': normal(ks[16], (DEPTH, D_MODEL, PEER_HEADS * PEER_QUERY_DIM), D_MODEL ** -0.5),
        'peer_sub_keys': normal(ks[17], (DEPTH, PEER_HEADS, 2, PEER_KEYS, PEER_QUERY_DIM // 2), (PEER_QUERY_DIM // 2) ** -0.5),
        'peer_down': normal(ks[18], (DEPTH, PEER_EXPERTS, D_MODEL), D_MODEL ** -0.5),
        'peer_up': normal(ks[19], (DEPTH, PEER_EXPERTS, D_MODEL), (PEER_HEADS * PEER_TOPK) ** -0.5),
    }

def reference(x, c, w_ada, b_ada, norm_pre_mix, norm_post_mix, norm_pre_ffn, norm_post_ffn,
              w_in, conv_w, a_log, dt_bias, dn_norm_w, w_attn_out, w_delta_out, w_mix_out,
              peer_w_query, peer_sub_keys, peer_down, peer_up):
    cond = jax.nn.silu(c)
    for layer in range(DEPTH):
        ada = cond @ w_ada[layer] + b_ada[layer]
        shift_m, scale_m, gate_m, shift_f, scale_f, gate_f = [t[:, None, :] for t in jnp.split(ada, 6, axis=-1)]
        h = rmsnorm(x, norm_pre_mix[layer]) * (1 + scale_m) + shift_m
        y = token_mixer(h, w_in[layer], conv_w[layer], a_log[layer], dt_bias[layer], dn_norm_w[layer],
                        w_attn_out[layer], w_delta_out[layer], w_mix_out[layer])
        x = x + gate_m * rmsnorm(y, norm_post_mix[layer])
        h = rmsnorm(x, norm_pre_ffn[layer]) * (1 + scale_f) + shift_f
        y = peer_ffn(h, peer_w_query[layer], peer_sub_keys[layer], peer_down[layer], peer_up[layer])
        x = x + gate_f * rmsnorm(y, norm_post_ffn[layer])
    return x


_drawn_inputs = setup_inputs


def setup_inputs(seed=0):
    import zlib

    import numpy as np

    out = dict(_drawn_inputs(seed))
    spreads = {}
    factors = {}
    for name, (base, spread) in spreads.items():
        noise = np.random.default_rng([zlib.crc32(name.encode()), seed]).standard_normal(out[name].shape)
        drawn = base * np.exp(spread * noise) if base else spread * noise
        out[name] = jnp.asarray(drawn.astype(out[name].dtype))
    for name, factor in factors.items():
        out[name] = (out[name] * factor).astype(out[name].dtype)
    return out
```

```python
from contextlib import ExitStack

import numpy as np

import concourse.bass as bass
from concourse import mybir

F32 = mybir.dt.float32
F32R = mybir.dt.float32r
U32 = mybir.dt.uint32
ALU = mybir.AluOpType
ACT = mybir.ActivationFunctionType
AX = mybir.AxisListType

P = 128
T = 512
TT = T // P
D = 2048
KT = D // P
AH, AG = 4, 3
NH = 16
PH = 8
TOPK = 16
NCHUNK = 128
LEVELS = 7
EPS = 1e-6
SCALE = float(P) ** -0.5
LOW = -3.0e38
ONE, DMA1 = 1, 16

U_ADA = 2 * KT
HALVES = 4 * 2 * KT
U_ATT = AH * AG * 3
U_GA = KT
U_WAO = 4
U_DN = NH * 4
U_GD = KT
U_WDO = KT
U_MIX = KT
U_Q = 3 * PH
U_TURN = 4
U_G = KT * 2
U_AFTER = 4
B_GA = U_ATT
B_WAO = B_GA + U_GA
B_DN = B_WAO + U_WAO
B_GD = B_DN + U_DN
B_WDO = B_GD + U_GD
B_MIX = B_WDO + U_WDO
B_Q = B_MIX + U_MIX
B_TURN = B_Q + U_Q
B_G = B_TURN + U_TURN
B_AFTER = B_G + U_G
B_PEER = B_AFTER + U_AFTER
EARLY = (2 * PH + U_TURN + U_G + U_AFTER) // 2
PAIRS = NCHUNK // 2
U_PEER = 4 * PAIRS - 2 * EARLY
EARLY_USES = EARLY // 2
ADA_USES = U_ADA // 4
SLOT_USES = B_PEER // 2
LOW_USES = SLOT_USES - 1
HIGH_USES = 1

V_BADA = 0
V_NORM = V_BADA + 6 * KT
V_CONV = V_NORM + 4 * KT
V_C = V_CONV + NH * 12
V_DNW = V_C + KT
V_AD = V_DNW + 1
V_N = V_AD + 2

C_ID = 0
C_NEG = C_ID + P
C_LEV = C_NEG + P
C_IOTA = C_LEV + LEVELS * P
C_N = C_IOTA + P
K_MASK = 0
K_COS = K_MASK + 10 * P
K_SIN = K_COS + T
K_PERM = K_SIN + T
K_N = K_PERM + 32

SHIFT_M, SCALE_M, GATE_M, SHIFT_F, SCALE_F, GATE_F = range(6)


class Steps:

    def __init__(self, eng, sem):
        self.eng, self.sem, self.base, self.n, self.total = eng, sem, 0, 0, 0

    def loop(self, i, per):
        self.total = self.base + self.n
        self.base, self.n, self.per = self.total + i * per, 0, per

    def end(self, times):
        assert self.n == self.per, (self.n, self.per)
        self.base, self.n = self.total + self.per * times, 0

    def __call__(self, ins):
        ins.then_inc(self.sem, 1)
        self.n += 1

    def sync(self):
        self.eng.wait_ge(self.sem, self.base + self.n)


def hybrid_block(nc, stream, ada_late, xT, vecs, consts, aconsts, wba, skz, gam_d, ga_d, x2_d, G_d, act_d, outT):
    with ExitStack() as ctx:
        offset = {}
        at = [nc.sbuf_base + (-nc.sbuf_base) % 64]

        def place(name, shape, dt, where=None):
            size = int(np.prod(shape[1:])) * 4
            if where is None:
                where = at[0]
                at[0] += size + (-size) % 64
            offset[name] = where
            return nc.alloc_sbuf_tensor_at(name, shape, dt, offset=where)

        def sem(name):
            return ctx.enter_context(nc.semaphore(name))

        bank = [ctx.enter_context(nc.psum_tensor(f"bank{i}", [P, T], F32)) for i in range(8)]
        bank4 = [b[:, :].rearrange("p (c n) -> p c n", c=4) for b in bank]

        raw = [place(f"raw{s}", [P, D], F32) for s in range(2)]
        hi = [place(f"hi{s}", [P, D], F32R) for s in range(2)]
        lo = [place(f"lo{s}", [P, D], F32R) for s in range(2)]
        xh = place("xh", [P, KT, T], F32R)
        xl = place("xl", [P, KT, T], F32R)
        R1 = place("R1", [P, KT, T], F32)
        R2 = place("R2", [P, KT, T], F32)
        r1, r2 = offset["R1"], offset["R2"]
        hi += [place(f"hi{s}", [P, D], F32R, r2 + (s - 2) * D * 8) for s in (2, 3)]
        lo += [place(f"lo{s}", [P, D], F32R, r2 + (s - 2) * D * 8 + D * 4) for s in (2, 3)]
        cst = place("cst", [P, C_N], F32)
        vec = place("vec", [P, V_N], F32)
        ones = place("ones", [P, P], F32)
        ada = place("ada", [P, 6 * KT], F32)
        cond = place("cond", [P, KT], F32)
        coef = place("coef", [P, 4, KT], F32)
        spare = place("spare", [P, 32], F32)
        eps = place("eps", [P, 2], F32)
        bycol = place("bycol", [P, TT, 48], F32)
        mcol = place("mcol", [P, 4], F32)
        acst = place("acst", [P, K_N], F32)
        tail = at[0]
        assert tail + 7 * T * 4 <= nc.sbuf_usable_end, (tail, nc.sbuf_usable_end)
        ident = cst[:, C_ID:C_ID + P]
        iota = cst[:, C_IOTA:C_IOTA + P]

        sq = [place(f"sq{s}", [P, T], F32, tail + s * T * 4) for s in range(2)]
        ssum = place("ssum", [P, T], F32, tail + 2 * T * 4)
        rs = place("rs", [P, T], F32, tail + 3 * T * 4)
        acc = place("acc", [P, D], F32, r2)
        wba_sb = place("wba_sb", [P, KT, 48], F32, r2 + D * 4)
        row = [place(f"row{s}", [48, T], F32, r2 + D * 4 + KT * 48 * 4 + s * T * 4) for s in range(4)]
        arow = raw + [place(f"arow{s}", [P, D], F32, offset[f"hi{s}"]) for s in range(2)]
        half = [place(f"half{s}", [P, D // 2], F32, tail + s * D * 2) for s in range(2)]
        hacc = [place(f"hacc{s}", [P, D // 2], F32, (r2 + 14 * T * 4, tail + 5 * T * 4)[s]) for s in range(2)]
        qk = [[place(f"qk{p}{j}", [P, T], F32, r2 + (p * 6 + j) * T * 4) for j in range(6)] for p in range(2)]
        vraw = [place(f"vraw{s}", [P, T], F32, r2 + (12 + s) * T * 4) for s in range(2)]
        YA = place("YA", [P, AH, T], F32, r1)
        vT = [[place(f"vT{p}{g}", [P, T], F32, r1 + (4 + p * 3 + g) * T * 4) for g in range(3)] for p in range(2)]
        prob = place("prob", [P, 10 * P], F32, r1 + 10 * T * 4)
        probT = place("probT", [P, 10 * P], F32, r1 + 13 * T * 4)
        yh = place("yh", [P, AH, T], F32R, r1 + 4 * T * 4)
        yl = place("yl", [P, AH, T], F32R, r1 + 8 * T * 4)
        rtmp = place("rtmp", [32, T], F32, tail + 4 * T * 4)
        spots = [r2 + n * T * 4 for n in range(16)] + [tail + n * T * 4 for n in range(7)]
        spots += [offset["acst"] + n * T * 4 for n in range(4)]

        def dn(name):
            return place("dn_" + name, [P, T], F32, spots.pop(0))

        dq, dk, dv, dz = zip(*[[dn(f"{x}{p}") for x in "qkvz"] for p in range(2)])
        (cv, th, dsq, drs, BG, BB, eg, dec, qks, LT, bt0, bt1, X, XT, T1, kdec, vb, qd) = [
            dn(x) for x in ("cv", "th", "sq", "rs", "BG", "BB", "eg", "dec", "qks", "LT", "bt0", "bt1",
                            "X", "XT", "T1", "kdec", "vb", "qd")]
        bt = [bt0, bt1]
        small = spots.pop(0)
        cw = place("dn_cw", [P, 12], F32, small)
        gcol = place("dn_gcol", [P, 4], F32, small + 64)
        bcol = place("dn_bcol", [P, 4], F32, small + 96)
        kcol = place("dn_kcol", [P, 4], F32, small + 128)
        egc = place("dn_egc", [P, 4], F32, small + 160)
        nbeg = place("dn_nbeg", [P, 4], F32, small + 192)
        dnw = place("dn_w", [P, 1], F32, small + 224)
        st_r = place("dn_r", [P, P], F32, small + 256)
        st_v = place("dn_v", [P, P], F32, small + 768)
        st_s = place("dn_s", [P, P], F32, small + 1280)

        skz_sb = place("skz_sb", [P, PH, 2 * P], F32, r1)
        I1, I2, GW = [place(n, [P, TT, P], F32, r2 + m * T * 4) for m, n in enumerate(("I1", "I2", "GW"))]
        qs = [place(f"qs{s}", [P, T], F32, r2 + (3 + s) * T * 4) for s in range(2)]
        Sc, Sc2, cand, cand2 = [place(n, [P, TT, 2 * P], F32, r2 + (5 + 2 * m) * T * 4)
                                for m, n in enumerate(("Sc", "Sc2", "cand", "cand2"))]
        pick = place("pick", [P, TT * TOPK, TOPK], F32, r2 + 13 * T * 4)
        hs = place("hs", [P, TT, 2, TOPK], F32, r2 + 15 * T * 4)
        hiu = place("hiu", [P, TT, 2, TOPK], U32, r2 + 15 * T * 4 + 512)
        hif = place("hif", [P, TT, 2, TOPK], F32, r2 + 15 * T * 4 + 1024)
        bs = place("bs", [P, TT, TOPK], F32, r2 + 15 * T * 4 + 1536)
        bp = place("bp", [P, TT, TOPK], U32, r2 + 15 * T * 4 + 1792)
        more = tail + 4 * T * 4
        be = place("be", [P, TT, TOPK], F32, more)
        pu = place("pu", [P, 2, TT * TOPK], U32, more + 256)
        pf = place("pf", [P, 2, TT * TOPK], F32, more + 768)
        pr = place("pr", [P, TT * TOPK], F32, more + 1280)
        bsum = place("bsum", [P, 2 * TT], F32, more + 1536)
        scrap = place("scrap", [P, 1], F32, more + 1568)
        i1T, i2T, gwT = [place(n, [P, T], F32, r2 + (3 + m) * T * 4) for m, n in enumerate(("i1T", "i2T", "gwT"))]
        hotA = [place(f"hotA{s}", [P, 8, P], F32, r2 + (6 + 2 * s) * T * 4) for s in range(2)]
        hotB = [place(f"hotB{s}", [P, 8, P], F32, r2 + (10 + 2 * s) * T * 4) for s in range(2)]
        stage = [place(f"stage{s}", [P, P, 32], F32, r1 + s * P * 32 * 4) for s in range(2)]
        spots = [offset["acst"] + n * T * 4 for n in range(4)] + [offset["cst"] + C_LEV * 4]
        cf2 = place("cf2", [P, 2, T], F32, spots.pop(0))
        spots.pop(0)
        cf = [cf2[:, j, :] for j in range(2)]
        etile = [place(f"etile{b}", [P, T], F32, tail + b * T * 4) for b in range(2)]
        elate = [place(f"elate{b}", [P, T], F32, tail + (2 + b) * T * 4) for b in range(2)]
        CH = [[place(f"CH{p}{j}", [P, T], F32R, tail + (2 * p + j) * T * 4) for j in range(2)] for p in range(2)]
        CL = [[None, place("CL01", [P, T], F32R, tail + 4 * T * 4)], [None, None]]
        CL[0][0] = place("CL00", [P, T], F32R, spots.pop(0))
        CL[1][0] = place("CL10", [P, T], F32R, spots.pop(0))
        CL[1][1] = place("CL11", [P, T], F32R, spots.pop(0))
        x2b = place("x2b", [P, KT, T], F32, offset["xh"])
        Gt = place("Gt", [P, 2, T], F32, tail + 5 * T * 4)

        raw_full = [sem(f"raw_full{s}") for s in range(2)]
        raw_used = [sem(f"raw_used{s}") for s in range(2)]
        arow_full = raw_full + [sem(f"arow_full{s}") for s in range(2)]
        arow_used = raw_used + [sem(f"arow_used{s}") for s in range(2)]
        half_full = [sem(f"half_full{s}") for s in range(2)]
        half_used = [sem(f"half_used{s}") for s in range(2)]
        hi_done = sem("hi_done")
        unit_done = [sem(f"unit_done{s}") for s in range(4)]
        bank_free = [sem(f"bank_free{s}") for s in range(2)]
        dve_step, act_step = sem("dve_step"), sem("act_step")
        s_in, s_x, s_const, s_tanh, s_cond = (sem("s_" + n) for n in ("in", "x", "const", "tanh", "cond"))
        s_adamm, s_ada = sem("s_adamm"), sem("s_ada")
        s_sq, s_ss, s_sum, s_rs, s_h, s_hi, s_lo, s_hr = (
            sem("s_" + n) for n in ("sq", "ss", "sum", "rs", "h", "hi", "lo", "hr"))
        s_turn, s_bycol = sem("s_turn"), sem("s_bycol")
        s_ba, s_rowb, s_rowa, s_row, s_rowd = (sem("s_" + n) for n in ("ba", "rowb", "rowa", "row", "rowd"))
        s_rot, s_rotd, s_vt, s_vtc, s_S, s_nm, s_exp, s_P, s_tr, s_pt, s_pv, s_ya = (
            sem("a_" + n) for n in ("rot", "rotd", "vt", "vtc", "S", "nm", "exp", "P", "tr", "pt", "pv", "ya"))
        s_yh, s_yl, s_wao, s_waoc, s_gad = (
            sem("a_" + n) for n in ("yh", "yl", "wao", "waoc", "gad"))
        d_sqe, d_sqo, d_sse, d_sso, d_rse, d_rso = (sem("d_" + n) for n in ("sqe", "sqo", "sse", "sso", "rse", "rso"))
        (d_th, d_e, d_nrm, d_bc, d_dd, d_kc, d_eg, d_dec, d_egc, d_p1, d_bt, d_x, d_kv,
         d_in, d_t1, d_t1c, d_xx, d_ks, d_r, d_v, d_vc, d_st, d_s, d_o, d_done, d_b0, d_b0t) = (
            sem("d_" + n) for n in (
                "th", "e", "nrm", "bc", "dd", "kc", "eg", "dec", "egc", "p1", "bt", "x",
                "kv", "in", "t1", "t1c", "xx", "ks", "r", "v", "vc", "st", "s", "o", "done", "b0", "b0t"))
        s_oh, s_ol, s_gal, s_mrg, s_mh, s_ml, s_xr, s_x2, s_x2d = (
            sem("m_" + n) for n in ("oh", "ol", "gal", "mrg", "mh", "ml", "xr", "x2", "x2d"))

        q_sk, q_sc, q_s, q_nb, q_e, q_done = (sem("q_" + n) for n in ("sk", "sc", "s", "nb", "e", "done"))
        g_tr, g_it, g_ab, g_mm, g_ev = (sem("g_" + n) for n in ("tr", "it", "ab", "mm", "ev"))
        g_dma = [sem(f"g_dma{s}") for s in range(2)]
        e_st = [sem(f"e_st{s}") for s in range(2)]
        p_act = sem("p_act")
        p_g, p_cf, p_ch, p_cl, p_y, p_add, s_x2l, s_out, s_stored = (
            sem("p_" + n) for n in ("g", "cf", "ch", "cl", "y", "add", "x2l", "out", "stored"))

        block = ctx.enter_context(nc.Block())


        sums_at = range(5, 5 + HALVES // 4, 4)

        def part(n):
            return ada[:, n * KT:(n + 1) * KT]

        def at_k(tile, k):
            return tile[:, k, :]

        def cc(tile, c):
            return tile[:, c * P:(c + 1) * P]

        def half_columns(x, lv, odd):
            return x.rearrange("p (b two s) -> p b two s", two=2, s=2 << lv)[:, :, odd, :]

        def packed(b, c, lv):
            return b[:, c * P // 2:(c + 1) * P // 2].rearrange("p (b s) -> p b s", s=2 << lv)

        def row_k(tile, n):
            if isinstance(n, int):
                return tile[:, n, :]
            return tile[:, bass.ds(n, 1), :].rearrange("p a t -> p (a t)")

        @block.sync
        def _(sp):
            sp.dma_start(R1[:, :, :], xT.rearrange("(k p) t -> p k t", p=P)).then_inc(s_x, 16)
            uses = ADA_USES + (B_PEER + U_PEER) // 2

            def load(i, s):
                sp.wait_ge(raw_used[s], i + ONE)
                sp.dma_start(raw[s][:, :],
                             stream[bass.ds(i * 2 + (s + U_ADA - 2 * ADA_USES), 1), :, :].rearrange("a p n -> (a p) n")
                             ).then_inc(raw_full[s], 16)

            def load_half(n, use, s):
                sp.wait_ge(half_used[s], use + ONE)
                sp.dma_start(half[s][:, :], ada_late[bass.ds(n, 1), :, :].rearrange("a p n -> (a p) n")
                             ).then_inc(half_full[s], 16)

            with sp.Fori(0, ADA_USES) as i:
                for s in range(4):
                    sp.wait_ge(arow_used[s], i + ONE)
                    sp.dma_start(arow[s][:, :], stream[bass.ds(i * 4 + s, 1), :, :].rearrange("a p n -> (a p) n")
                                 ).then_inc(arow_full[s], 16)
            for s in range(2):
                load(ADA_USES, s)
            sp.wait_ge(s_h, KT)
            with sp.Fori(0, HALVES // 8) as i:
                for s in range(2):
                    for j in range(4):
                        if j == 2:
                            load(i + (ADA_USES + 1), s)
                        load_half(i * 8 + (s * 4 + j), i * 4 + (s * 2 + j // 2), j % 2)
            with sp.Fori(ADA_USES + 1 + HALVES // 8, uses) as i:
                for s in range(2):
                    load(i, s)
            for k in range(KT):
                sp.wait_ge(s_out, k + 1)
                sp.dma_start(outT[k * P:(k + 1) * P, :], R1[:, k, :]).then_inc(s_stored, 16)
            sp.wait_ge(s_stored, KT * 16)

        @block.gpsimd
        def _(pool):
            def split(s, slot, landed, free, count):
                pool.wait_ge(raw_full[s], landed)
                if free is not None:
                    pool.wait_ge(unit_done[slot], free + ONE)
                nc.gpsimd.tensor_tensor(hi[slot][:, :], raw[s][:, :], ones[:, 0:1].to_broadcast([P, D]), ALU.mult
                                        ).then_inc(hi_done, 1)
                pool.wait_ge(hi_done, count)
                nc.gpsimd.tensor_tensor(lo[slot][:, :], raw[s][:, :], hi[slot][:, :].bitcast(F32),
                                        ALU.subtract).then_inc(raw_used[s], 1)

            pool.wait_ge(s_const, 1)
            for s in (2, 3):
                pool.wait_ge(arow_used[s], ADA_USES + ONE)
            with pool.Fori(0, LOW_USES) as i:
                for s in range(2):
                    split(s, s, (ADA_USES + 1 + i) * 16, i, i * 2 + s + 1)
            pool.wait_ge(g_mm, T // 8 + ONE)
            for s in range(2):
                split(s, 2 + s, (ADA_USES + SLOT_USES) * 16, None, B_PEER - 1 + s)
            with pool.Fori(0, U_PEER // 4) as i:
                for q in range(4):
                    split(q % 2, q, (ADA_USES + SLOT_USES + q // 2 + 1 + i * 2) * 16,
                          i + (LOW_USES if q < 2 else HIGH_USES), i * 4 + (B_PEER + q + 1))

        @block.tensor
        def _(pe):
            def product(slot, use, out, between=None, bank_use=None, ready=None):
                pe.wait_ge(raw_used[slot % 2], use + (ADA_USES + 1) + ONE)
                pe.wait_ge(bank_free[slot % 2], use if bank_use is None else bank_use)
                for k in range(KT):
                    w = slice(k * P, (k + 1) * P)
                    if ready:
                        pe.wait_ge(ready[0], ready[1] + k + 1)
                    nc.tensor.matmul(out, hi[slot][:, w], at_k(xh, k), start=(k == 0), stop=False,
                                     skip_group_check=True)
                    nc.tensor.matmul(out, hi[slot][:, w], at_k(xl, k), start=False, stop=False,
                                     skip_group_check=True)
                    mm = nc.tensor.matmul(out, lo[slot][:, w], at_k(xh, k), start=False, stop=(k == KT - 1),
                                          skip_group_check=True)
                    if k == KT - 1:
                        mm.then_inc(unit_done[slot], 1)
                    if between:
                        between(k)

            def norm_tile(n, k, out):
                pe.wait_ge(s_sq, n * KT + k + 1)
                nc.tensor.matmul(out[:, :], ones[:, :], sq[k % 2][:, :], start=(k == 0), stop=(k == KT - 1),
                                 skip_group_check=True).then_inc(s_ss, 1)

            pe.wait_ge(s_const, 1)
            for k in range(KT):
                norm_tile(0, k, bank[7])
            with pe.Fori(0, 2) as c:
                pe.wait_ge(arow_used[3], (c + 1) * (KT // 4) + ONE)
                for n in range(KT):
                    mm = nc.tensor.matmul(bank[0][:, n:n + 1], acc[:, n * P:(n + 1) * P], ones[:, 0:1],
                                          start=True, stop=True, skip_group_check=True)
                mm.then_inc(s_adamm, 1)
                pe.wait_ge(s_ada, c + 1)
            def rows_between(u, k):
                if u == 0 and k == 0:
                    pe.wait_ge(s_in, 64)
                if u == 0 and k or u == 1 and k == 0:
                    r = u * KT + k - 1
                    pe.wait_ge(s_hr, r + 1)
                    mm = nc.tensor.matmul(bank[2][0:48, :], wba_sb[:, r, :], at_k(R1, r), start=(r == 0),
                                          stop=(r == KT - 1), skip_group_check=True)
                    if r == KT - 1:
                        mm.then_inc(s_ba, 1)
                if u == 2 and k == 1:
                    pe.wait_ge(s_row, 1)
                    for c in range(TT):
                        mm = nc.tensor.transpose(bank4[3][:, c, 0:48], cc(row[1], c), cst[0:48, C_ID:C_ID + 48])
                    mm.then_inc(s_turn, 1)

            turned = [0]
            summed = [2]

            def sum_late(q):
                pe.wait_ge(half_used[1], (q + 1) * (KT // 2) + ONE)
                if turned[0]:
                    pe.wait_ge(s_vtc, turned[0])
                for n in range(KT // 2):
                    mm = nc.tensor.matmul(bank[3][:, n:n + 1], hacc[q % 2][:, n * P:(n + 1) * P], ones[:, 0:1],
                                          start=True, stop=True, skip_group_check=True)
                mm.then_inc(s_adamm, 1)
                summed[0] += 1

            def swap_halves(h, a):
                n, u = h * 6 + (a // 3) * 2 + a % 3, h * 9 + a
                pe.wait_ge(bank_free[u % 2], u // 2 + 1)
                if n >= 1:
                    pe.wait_ge(s_rotd, n)
                else:
                    pe.wait_ge(s_rowb, 1)
                nc.tensor.matmul(bank[2][0:32, :], acst[0:32, K_PERM:K_PERM + 32],
                                 qk[h % 2][(a // 3) * 2 + a % 3][0:32, :], start=True, stop=True).then_inc(s_rot, 1)

            def turn_v(h, g):
                u, n = h * 9 + g * 3 + 2, h * 3 + g
                pe.wait_ge(bank_free[u % 2], u // 2 + 1)
                if n >= 1:
                    pe.wait_ge(s_vtc, n)
                else:
                    pe.wait_ge(s_bycol, 1)
                pe.wait_ge(s_ada, summed[0])
                for c in range(4):
                    mm = nc.tensor.transpose(bank4[3][:, c, :], cc(vraw[n % 2], c), ident)
                mm.then_inc(s_vt, 1)
                turned[0] += 1

            def blocks(i):
                return [(0, j) for j in range(max(i - 1, 0), i + 1)] + [(g, j) for g in (1, 2) for j in range(i + 1)]

            def scores(h, i):
                t = h * 4 + i
                pe.wait_ge(s_rotd, 6 * (h + 1))
                if t >= 1:
                    pe.wait_ge(s_pt, t)
                for g in range(AG):
                    js = [j for gg, j in blocks(i) if gg == g]
                    mm = nc.tensor.matmul(bank[4 + g][:, 0:len(js) * P], cc(qk[h % 2][2 * g], i),
                                          qk[h % 2][2 * g + 1][:, js[0] * P:(js[-1] + 1) * P], start=True, stop=True)
                mm.then_inc(s_S, 1)

            def turn_probs(h, i):
                t = h * 4 + i
                pe.wait_ge(s_P, t + 1)
                for b in range(len(blocks(i))):
                    mm = nc.tensor.transpose(bank4[4 + b // 4][:, b % 4, :], cc(prob, b), ident)
                mm.then_inc(s_tr, 1)

            def values(h, i):
                t = h * 4 + i
                pe.wait_ge(s_pt, t + 1)
                pe.wait_ge(s_vtc, 3 * (h + 1))
                if h >= 1 and i == 0:
                    pe.wait_ge(s_ya, h)
                bl = blocks(i)
                for b, (g, j) in enumerate(bl):
                    mm = nc.tensor.matmul(bank4[7][:, i, :], cc(vT[h % 2][g], j), cc(probT, b),
                                          start=(b == 0), stop=(b == len(bl) - 1), skip_group_check=True)
                mm.then_inc(s_pv, 1)

            def attention_between(h, a):
                def step(k):
                    if h == 0 and a < 3:
                        rows_between(a, k)
                    if k == 1 and h * 9 + a in sums_at:
                        sum_late(sums_at.index(h * 9 + a))
                    if k == 8 and a >= 1 and (a - 1) % 3 < 2:
                        swap_halves(h, a - 1)
                    if k == 8 and a >= 1 and (a - 1) % 3 == 2:
                        turn_v(h, (a - 1) // 3)
                    if h >= 1:
                        if a == 0 and k == 2:
                            turn_v(h - 1, 2)
                        if a < 8 and a % 2 == 0 and k == 5:
                            scores(h - 1, a // 2)
                        if a < 8 and a % 2 == 1 and k == 0:
                            turn_probs(h - 1, a // 2)
                        if a < 8 and a % 2 == 1 and k == 12:
                            values(h - 1, a // 2)
                return step

            for h in range(AH):
                for a in range(9):
                    u = h * 9 + a
                    product(u % 2, u // 2, bank[u % 2][:, :], attention_between(h, a),
                            ready=None if u else (s_lo, 0))
            def last_between(n):
                def step(k):
                    if n == 0 and k == 2:
                        turn_v(AH - 1, 2)
                    if n < TT and k == 4:
                        scores(AH - 1, n)
                    if 1 <= n <= TT and k == 0:
                        turn_probs(AH - 1, n - 1)
                    if 1 <= n <= TT and k == 10:
                        values(AH - 1, n - 1)
                return step

            for n in range(6):
                product(n % 2, (B_GA + n) // 2, bank[n % 2][:, :], last_between(n))
            with pe.Fori(3, U_GA // 2) as i:
                for s in range(2):
                    product(s, i + B_GA // 2, bank[s][:, :])
            pe.wait_ge(s_yl, 1)
            for w in range(U_WAO):
                u = B_WAO + w
                pe.wait_ge(raw_used[u % 2], ADA_USES + u // 2 + 1 + ONE)
                if w >= 1:
                    pe.wait_ge(s_waoc, 3 * w)
                    pe.wait_ge(bank_free[(u - 1) % 2], (u - 1) // 2 + 1)
                for n in range(4):
                    for k in range(AH):
                        c = slice((n * AH + k) * P, (n * AH + k + 1) * P)
                        nc.tensor.matmul(bank[2 + n][:, :], hi[u % 2][:, c], yh[:, k, :], start=(k == 0),
                                         stop=False, skip_group_check=True)
                        nc.tensor.matmul(bank[2 + n][:, :], hi[u % 2][:, c], yl[:, k, :], start=False,
                                         stop=False, skip_group_check=True)
                        mm = nc.tensor.matmul(bank[2 + n][:, :], lo[u % 2][:, c], yh[:, k, :], start=False,
                                              stop=(k == AH - 1), skip_group_check=True)
                    if n < 3:
                        mm.then_inc(s_wao, 1)
                mm.then_inc(unit_done[u % 2], 1)

            def delta_steps(h, p, j, k):
                h2 = h * 2 + 4 if not (isinstance(h, int) and h == NH - 1) else 2 * NH
                if j == 0 and k == 0:
                    pe.wait_ge(d_nrm, h * 2 + 2)
                    for c in range(4):
                        mm = nc.tensor.matmul(bank4[3][:, c, :], cc(dk[p], c), cc(dq[p], c), start=True, stop=True,
                                              skip_group_check=True)
                    mm.then_inc(d_p1, 1)
                    for c in range(4):
                        mm = nc.tensor.matmul(bank4[4][:, c, :], cc(dk[p], c), cc(dk[p], c), start=True, stop=True,
                                              skip_group_check=True)
                    mm.then_inc(d_p1, 1)
                    for c in range(4):
                        mm = nc.tensor.transpose(bank4[5][:, c, :], cc(dk[p], c), ident)
                    mm.then_inc(d_p1, 1)
                    pe.wait_ge(d_e, h * 3 + 3)
                    for c in range(4):
                        mm = nc.tensor.transpose(bank4[6][:, c, :], cc(dv[p], c), ident)
                    mm.then_inc(d_p1, 1)
                if j == 0 and k == 12:
                    pe.wait_ge(d_b0, h + 1)
                    for c in range(4):
                        mm = nc.tensor.transpose(bank4[3][:, c, :], cc(bt[0], c), ident)
                    mm.then_inc(d_b0t, 1)
                if j in (1, 2) and k in (0, 6, 11):
                    lv = 3 * (j - 1) + (0, 6, 11).index(k)
                    pe.wait_ge(d_x, h * LEVELS + lv + 1)
                    pe.wait_ge(d_bt, h * (LEVELS - 1) + lv + 1)
                    for c in range(4):
                        mm = nc.tensor.matmul(bank4[4][:, c, :], cc(bt[(lv + 1) % 2], c), cc(X, c), start=True,
                                              stop=True, skip_group_check=True)
                    mm.then_inc(d_t1, 1)
                if j in (1, 2) and k in (2, 8, 13):
                    lv = 3 * (j - 1) + (2, 8, 13).index(k)
                    pe.wait_ge(d_t1c, h * (LEVELS - 1) + lv + 1)
                    if lv < LEVELS - 2:
                        for c in range(4):
                            nc.tensor.matmul(packed(bank[5], c, lv), cc(XT, c), half_columns(cc(T1, c), lv, 0),
                                             start=True, stop=True, skip_group_check=True)
                    for c in range(4):
                        mm = nc.tensor.matmul(packed(bank[6], c, lv), cc(T1, c), half_columns(cc(XT, c), lv, 1),
                                              start=True, stop=True, skip_group_check=True)
                    mm.then_inc(d_xx, 1)
                if j == 3 and (k < 3 or 6 <= k < 15):
                    c, what = (0, k) if k < 3 else (k // 3 - 1, k % 3)
                    if what == 0 and c == 0:
                        pe.wait_ge(d_x, h * LEVELS + LEVELS)
                        pe.wait_ge(d_kv, h + 1)
                    if what == 0 and c > 0:
                        pe.wait_ge(d_s, h * 3 + c)
                        nc.tensor.matmul(bank[3][:, 0:P], cc(dk[p], c), st_s[:, :], start=True,
                                         stop=True).then_inc(d_ks, 1)
                    if what == 1:
                        if c > 0:
                            pe.wait_ge(d_r, h * 3 + c)
                        nc.tensor.matmul(bank[4][:, 0:P], cc(XT, c), st_r[:, :] if c else cc(vb, 0), start=True,
                                         stop=True).then_inc(d_v, 1)
                    if what == 2:
                        pe.wait_ge(d_vc, h * 4 + c + 1)
                        if c == 0:
                            pe.wait_ge(d_in, h + 1)
                            pe.wait_ge(d_done, h + ONE)
                        else:
                            nc.tensor.matmul(bank4[7][:, c, :], st_s[:, :], cc(qd, c), start=True, stop=False,
                                             skip_group_check=True)
                        mm = nc.tensor.matmul(bank4[7][:, c, :], st_v[:, :], cc(qks, c), start=(c == 0), stop=True,
                                              skip_group_check=True)
                        if c < 3:
                            nc.tensor.matmul(bank[5][:, 0:P], cc(kdec, c), st_v[:, :], start=True,
                                             stop=True).then_inc(d_st, 1)
                        else:
                            mm.then_inc(d_o, 1)
                if j == 3 and k == 15:
                    pe.wait_ge(d_sqo, h + 1)
                    pe.wait_ge(d_rse, h2)
                    nc.tensor.matmul(bank[2][:, :], ones[:, :], dsq[:, :], start=True, stop=True).then_inc(d_sso, 1)

            def norm_steps(h, j, k):
                if k == 14 and j == 1:
                    if not (isinstance(h, int) and h == 0):
                        pe.wait_ge(d_rso, h - 1 + ONE)
                    pe.wait_ge(d_sqe, h * 2 + 1)
                    nc.tensor.matmul(bank[2][:, :], ones[:, :], dsq[:, :], start=True, stop=True).then_inc(d_sse, 1)
                if k == 14 and j == 2:
                    pe.wait_ge(d_rse, h * 2 + 1)
                    pe.wait_ge(d_sqe, h * 2 + 2)
                    nc.tensor.matmul(bank[2][:, :], ones[:, :], dsq[:, :], start=True, stop=True).then_inc(d_sse, 1)

            def delta_head(h, p):
                for j in range(4):
                    def step(k, j=j):
                        if not (isinstance(h, int) and h == 0):
                            delta_steps(h - 1, 1 - p, j, k)
                        norm_steps(h, j, k)
                    product(j % 2, h * 2 + (B_DN // 2 + j // 2), bank[j % 2][:, :], step)

            delta_head(0, 0)
            with pe.Fori(0, NH // 2 - 1) as i:
                delta_head(i * 2 + 1, 1)
                delta_head(i * 2 + 2, 0)
            delta_head(NH - 1, 1)
            for j in range(4):
                product(j % 2, B_GD // 2 + j // 2, bank[j % 2][:, :], lambda k, j=j: delta_steps(NH - 1, 1, j, k))
            with pe.Fori(2, U_GD // 2) as i:
                for s in range(2):
                    product(s, i + B_GD // 2, bank[s][:, :])
            for base, split in ((B_WDO, s_ol), (B_MIX, s_ml)):
                for s in range(2):
                    product(s, base // 2, bank[s][:, :], ready=None if s else (split, 0))
                with pe.Fori(1, KT // 2) as i:
                    for s in range(2):
                        product(s, i + base // 2, bank[s][:, :])
            pe.wait_ge(s_ss, 2 * KT)
            nc.tensor.matmul(bank[7][:, :], ones[:, :], ssum[:, :], start=True, stop=True).then_inc(s_sum, 1)
            pe.wait_ge(s_rs, 2)
            for k in range(KT):
                norm_tile(2, k, bank[7])
            def scores_of(s, h, queries):
                def step(k):
                    if k == 3:
                        pe.wait_ge(bank_free[s], queries)
                        pe.wait_ge(q_sk, 16)
                        pe.wait_ge(q_s, h + ONE)
                        for t in range(TT):
                            mm = nc.tensor.matmul(bank[2 + t // 2][:, t % 2 * 256:t % 2 * 256 + 256],
                                                  cc(qs[s], t),
                                                  skz_sb[:, bass.ds(h, 1), :].rearrange("p a n -> p (a n)"),
                                                  start=True, stop=True, skip_group_check=True)
                        mm.then_inc(q_sc, 1)
                return step

            def two_heads(i, first=False):
                for s in range(2):
                    for n in range(3):
                        u = 3 * s + n
                        product(u % 2, i * 3 + (B_Q // 2 + u // 2), bank[u % 2][:, :],
                                scores_of(s, i * 2 + s, i * 3 + (B_Q // 2 + (3 * s) // 2 + 1)) if n == 1 else None,
                                ready=(s_lo, KT) if first and u == 0 else None)

            two_heads(0, True)
            with pe.Fori(1, PH // 2) as i:
                two_heads(i)
            def turn_choices(k):
                if k == 8:
                    pe.wait_ge(q_done, PH + ONE)
                    pe.wait_ge(q_s, PH + ONE)
                    for n, src in enumerate((I1, I2, GW)):
                        for t in range(TT):
                            mm = nc.tensor.transpose(bank4[2 + n][:, t, :], src[:, t, :], ident)
                        mm.then_inc(g_tr, 1)

            for j in range(U_TURN):
                product(j % 2, B_TURN // 2 + j // 2, bank[j % 2][:, :], turn_choices if j == 2 else None)
            pe.wait_ge(g_it, 3)
            def token_weights(i, j):
                def step(k):
                    if k not in (7, KT - 1):
                        return
                    n = 2 * j + k // 8
                    pe.wait_ge(g_ab, i * 8 + n + 1)
                    pe.wait_ge(g_ev, i * 8 + max(n - 1, 0) + ONE)
                    for t in range(8):
                        mm = nc.tensor.matmul(bank4[2 + 2 * (n % 2) + t // 4][:, t % 4, :], hotB[n % 2][:, t, :],
                                              hotA[n % 2][:, t, :], start=True, stop=True, skip_group_check=True)
                    mm.then_inc(g_mm, 1)
                return step

            with pe.Fori(0, T // 64) as i:
                for j in range(4):
                    product(j % 2, i * 2 + (B_G // 2 + j // 2), bank[j % 2][:, :], token_weights(i, j))
            for j in range(U_AFTER):
                product(j, B_AFTER // 2 + j // 2, bank[j % 2][:, :])
            def up(m, slots, raw_use, par, last=False):
                for j in range(2):
                    pe.wait_ge(raw_used[j], raw_use + (ADA_USES + 1) + ONE)
                pe.wait_ge(p_cl, m * 2 + 2 + ONE)
                for n in range(KT):
                    pe.wait_ge(p_add, m * KT + max(n - 5, 0) + ONE)
                    w = slice(n * P, (n + 1) * P)
                    for j in range(2):
                        y = bank[2 + n % 6][:, :]
                        nc.tensor.matmul(y, hi[slots[j]][:, w], CH[par][j][:, :], start=(j == 0), stop=False,
                                         skip_group_check=True)
                        nc.tensor.matmul(y, hi[slots[j]][:, w], CL[par][j][:, :], start=False, stop=False,
                                         skip_group_check=True)
                        mm = nc.tensor.matmul(y, lo[slots[j]][:, w], CH[par][j][:, :], start=False, stop=(j == 1),
                                              skip_group_check=True)
                        if n == KT - 1:
                            mm.then_inc(unit_done[slots[j]], 1)
                        elif j == 1:
                            mm.then_inc(p_y, 1)
                    if last and n >= 3:
                        norm_tile(3, n - 3, bank[0])

            with pe.Fori(0, EARLY // 2) as i:
                for e in range(2):
                    up(i * 2 + e, (2 * e, 2 * e + 1), i * 2 + (SLOT_USES + e), e)
            R = SLOT_USES + EARLY
            for j in range(2):
                product(j, R, bank[j][:, :], bank_use=SLOT_USES)
            with pe.Fori(0, (PAIRS - EARLY) // 2 - 1) as i:
                for e in range(2):
                    for j in range(2):
                        product(2 + j, i * 4 + (R + 1 + 2 * e), bank[j][:, :], bank_use=i * 2 + (SLOT_USES + 1 + e))
                    up(i * 2 + (EARLY + e), (0, 1), i * 4 + (R + 2 + 2 * e), e)
            m = PAIRS - EARLY - 2
            for j in range(2):
                product(2 + j, R + 1 + 2 * m, bank[j][:, :], bank_use=SLOT_USES + 1 + m)
            up(PAIRS - 2, (0, 1), R + 2 + 2 * m, 0)
            up(PAIRS - 1, (2, 3), R + 1 + 2 * (m + 1), 1, True)
            for k in range(KT - 3, KT):
                norm_tile(3, k, bank[0])

        @block.scalar
        def _(act):
            step = Steps(act, act_step)
            act.dma_start(vec[:, :], vecs).then_inc(s_in, 16)
            act.dma_start(cst[:, :], consts).then_inc(s_in, 16)
            act.dma_start(acst[:, :], aconsts).then_inc(s_in, 16)
            act.dma_start(wba_sb[:, :, :], wba).then_inc(s_in, 16)
            act.wait_ge(s_const, 1)
            act.wait_ge(s_in, 64)
            nc.scalar.activation(cond[:, :], vec[:, V_C:V_C + KT], ACT.Tanh, scale=0.5).then_inc(s_tanh, 1)

            def squares(n, x):
                for k in range(KT):
                    if n or k > 1:
                        act.wait_ge(s_ss, n * KT + k - 1)
                    nc.scalar.activation(sq[k % 2][:, :], x(k), ACT.Square).then_inc(s_sq, 1)

            def inverse_root(n, out=bank[7]):
                if n == 1:
                    act.wait_ge(s_sum, 1)
                else:
                    act.wait_ge(s_ss, (n + 1) * KT)
                step(nc.scalar.activation(rs[:, :], out[:, :], ACT.Ln, bias=eps[:, 0:1], scale=1.0 / D))
                step.sync()
                nc.scalar.activation(rs[:, :], rs[:, :], ACT.Exp, scale=-0.5).then_inc(s_rs, 1)

            def shifted(k, dst, src, shift, done):
                nc.scalar.activation(dst[:, k, :], src[:, k, :], ACT.Identity, bias=shift[:, k:k + 1]
                                     ).then_inc(done, 1)

            act.wait_ge(s_x, 16)
            squares(0, lambda k: at_k(R1, k))
            inverse_root(0)
            for k in range(KT + 1):
                if k < KT:
                    act.wait_ge(s_h, k + 1)
                    shifted(k, xh, R1, part(SHIFT_M), s_hi)
                if k:
                    act.wait_ge(s_lo, k)
                    shifted(k - 1, R1, R1, part(SHIFT_M), s_hr)

            def rows():
                act.wait_ge(s_ba, 1)
                nc.scalar.activation(row[0][0:16, :], bank[2][0:16, :], ACT.Tanh, scale=0.5).then_inc(s_rowa, 1)
                act.wait_ge(s_rowb, 1)
                step(nc.scalar.activation(row[2][32:48, :], row[2][32:48, :], ACT.Exp, scale=-1.0))
                step.sync()
                step(nc.scalar.activation(row[2][32:48, :], row[2][32:48, :], ACT.Ln, bias=eps[32:48, 1:2]))
                step(nc.scalar.activation(row[3][32:48, 0:1], vec[32:48, V_AD:V_AD + 1], ACT.Exp))
                step.sync()
                nc.scalar.activation(row[3][32:48, 1:2], row[3][32:48, 0:1], ACT.Copy, scale=-1.0).then_inc(s_rowa, 1)
                act.wait_ge(s_row, 1)
                act.dma_start(gam_d[0:16, :], row[1][0:16, :]).then_inc(s_rowd, 16)
                act.dma_start(gam_d[16:32, :], row[1][32:48, :]).then_inc(s_rowd, 16)

            def copy_vt(h, g):
                n = h * 3 + g
                act.wait_ge(s_vt, n + 1)
                nc.scalar.activation(vT[h % 2][g][:, :], bank[3][:, :], ACT.Copy).then_inc(s_vtc, 1)

            def exps(h, i):
                t = h * 4 + i
                n = ((1 if i == 0 else 2) + 2 * (i + 1)) * P
                act.wait_ge(s_nm, t + 1)
                nc.scalar.activation(prob[:, 0:n], prob[:, 0:n], ACT.Exp, bias=mcol[:, 0:1],
                                     accum_out=mcol[:, 1:2]).then_inc(s_exp, 1)

            def copy_pt(h, i):
                t = h * 4 + i
                n = (1 if i == 0 else 2) + 2 * (i + 1)
                act.wait_ge(s_tr, t + 1)
                if t >= 1:
                    act.wait_ge(s_pv, t)
                m = range((n + 3) // 4)
                for b in m:
                    w = min(4, n - 4 * b) * P
                    ins = nc.scalar.activation(probT[:, b * T:b * T + w], bank[4 + b][:, 0:w], ACT.Copy)
                ins.then_inc(s_pt, 1)

            def copy_ya(h):
                act.wait_ge(s_pv, 4 * (h + 1))
                nc.scalar.activation(YA[:, h, :], bank[7][:, :], ACT.Copy).then_inc(s_ya, 1)

            for h in range(AH):
                for a in range(9):
                    u = h * 9 + a
                    if h >= 1 and a == 0:
                        copy_vt(h - 1, 2)
                    if a >= 1 and (a - 1) % 3 == 2:
                        copy_vt(h, (a - 1) // 3)
                    if h >= 1 and a < 8:
                        (exps if a % 2 == 0 else copy_pt)(h - 1, a // 2)
                    if h >= 1 and a == 8:
                        copy_ya(h - 1)
                    g, j = a // 3, a % 3
                    dst = qk[h % 2][2 * g + j] if j < 2 else vraw[(h * 3 + g) % 2]
                    act.wait_ge(unit_done[u % 2], u // 2 + 1 + ONE)
                    nc.scalar.activation(dst[:, :], bank[u % 2][:, :], ACT.Copy).then_inc(bank_free[u % 2], 1)
                    if u == 0:
                        rows()
                    if u == 2:
                        act.wait_ge(s_rowd, 32)
            def gate(i, s):
                act.wait_ge(unit_done[s], i + (B_GA // 2 + 1) + ONE)
                nc.scalar.activation(row_k(R2, i * 2 + s), bank[s][:, :], ACT.Tanh, scale=0.5
                                     ).then_inc(bank_free[s], 1)

            copy_vt(AH - 1, 2)
            for n in range(6):
                if 1 <= n <= TT:
                    copy_pt(AH - 1, n - 1)
                if n < TT:
                    exps(AH - 1, n)
                if n == TT:
                    copy_ya(AH - 1)
                    act.wait_ge(s_ya, AH)
                    nc.scalar.activation(yh[:, :, :], YA[:, :, :], ACT.Copy).then_inc(s_yh, 1)
                gate(n // 2, n % 2)
            with act.Fori(3, U_GA // 2) as i:
                for s in range(2):
                    gate(i, s)
            act.wait_ge(s_waoc, 3 * U_WAO)
            for s in range(2):
                act.wait_ge(bank_free[s], B_DN // 2)
            act.dma_start(ga_d, R2[:, :, :]).then_inc(s_gad, 16)
            act.wait_ge(s_gad, 16)

            def load_rows(h):
                act.dma_start(BG[:, :], gam_d[bass.ds(h + 16, 1), :].broadcast_to([P, T])).then_inc(d_bc, 16)
                act.dma_start(BB[:, :], gam_d[bass.ds(h, 1), :].broadcast_to([P, T])).then_inc(d_bc, 16)

            def root_of(scale, done):
                step(nc.scalar.activation(drs[:, :], bank[2][:, :], ACT.Ln, bias=eps[:, 0:1], scale=scale))
                step.sync()
                nc.scalar.activation(drs[:, :], drs[:, :], ACT.Exp, scale=-0.5).then_inc(done, 1)

            def root_qk(h, j):
                act.wait_ge(d_sse, h * 2 + j + 1)
                if j:
                    act.wait_ge(d_nrm, h * 2 + 1)
                elif not (isinstance(h, int) and h == 0):
                    act.wait_ge(d_done, h - 1 + ONE)
                root_of(1.0, d_rse)

            def root_out(h):
                act.wait_ge(d_sso, h + 1 + ONE)
                act.wait_ge(d_nrm, 2 * NH if isinstance(h, int) and h == NH - 1 else h * 2 + 4)
                root_of(1.0 / P, d_rso)

            def copy_level(h, lv):
                act.wait_ge(d_t1, h * (LEVELS - 1) + lv + 1)
                nc.scalar.activation(T1[:, :], bank[4][:, :], ACT.Copy).then_inc(d_t1c, 1)

            def copy_values(h, c):
                act.wait_ge(d_v, h * 4 + c + 1)
                nc.scalar.activation(st_v[:, :], bank[4][:, 0:P], ACT.Copy).then_inc(d_vc, 1)

            def ahead_of_unit(h, j):
                if j < 2:
                    copy_level(h, 3 * j)
                if j == 2:
                    copy_values(h, 0)

            def delta_part(h, p, j):
                if j == 0:
                    act.wait_ge(d_bc, (h + 1) * 32)
                    nc.scalar.activation(eg[:, :], BG[:, :], ACT.Exp).then_inc(d_eg, 1)
                    act.wait_ge(d_dd, h + 1)
                    nc.scalar.activation(dec[:, :], dec[:, :], ACT.Exp).then_inc(d_dec, 1)
                    act.wait_ge(d_kc, h + 1)
                    step(nc.scalar.activation(kcol[:, :], kcol[:, :], ACT.Exp))
                    nc.scalar.activation(egc[:, :], gcol[:, :], ACT.Exp).then_inc(d_egc, 1)
                    step.sync()
                    act.wait_ge(d_p1, h * 4 + 4)
                    for c in range(4):
                        nc.scalar.activation(cc(kdec, c), bank4[5][:, c, :], ACT.Copy, scale=kcol[:, c:c + 1])
                    for c in range(4):
                        ins = nc.scalar.activation(cc(vb, c), bank4[6][:, c, :], ACT.Copy, scale=bcol[:, c:c + 1])
                    ins.then_inc(d_kv, 1)
                    act.wait_ge(d_kv, h + 1)
                    act.wait_ge(d_b0, h + 1)
                    if isinstance(h, int) and h == NH - 1:
                        return
                    load_rows(h + 1)
                if j in (1, 2):
                    for lv in range(3 * j - 2, 3 * j):
                        copy_level(h, lv)
                if j == 3:
                    for c in range(1, 4):
                        copy_values(h, c)
                    act.wait_ge(d_o, h + 1)
                    act.wait_ge(d_sse, 2 * NH if isinstance(h, int) and h == NH - 1 else h * 2 + 4)
                    nc.scalar.activation(dsq[:, :], bank[7][:, :], ACT.Square).then_inc(d_sqo, 1)

            def delta_units(h, p):
                first = isinstance(h, int) and h == 0
                for j in range(4):
                    if not first:
                        delta_part(h - 1, 1 - p, j)
                    if j in (1, 2):
                        root_qk(h, j - 1)
                    if j == 0:
                        act.wait_ge(bank_free[1], h * 2 + B_DN // 2)
                    if not first:
                        ahead_of_unit(h - 1, j)
                    if j < 3:
                        act.wait_ge(d_e, h * 3 + j)
                        act.wait_ge(bank_free[j % 2], h * 2 + (B_DN // 2 + j // 2 + 1))
                        nc.scalar.activation(th[:, :], cv[:, :], ACT.Tanh).then_inc(d_th, 1)
                    else:
                        act.wait_ge(d_e, h * 3 + 3)
                        act.wait_ge(unit_done[1], h * 2 + (B_DN // 2 + 2) + ONE)
                        nc.scalar.activation(th[:, :], bank[1][:, :], ACT.Tanh, scale=0.5).then_inc(d_th, 1)
                    if j < 2:
                        act.wait_ge(d_e, h * 3 + j + 1)
                        if j:
                            act.wait_ge(d_sse, h * 2 + 1)
                        elif not first:
                            act.wait_ge(d_sso, h - 1 + ONE)
                        nc.scalar.activation(dsq[:, :], (dq, dk)[j][p][:, :], ACT.Square).then_inc(d_sqe, 1)
                    if j == 3 and not first:
                        root_out(h - 1)

            load_rows(0)
            delta_units(0, 0)
            with act.Fori(0, NH // 2 - 1) as i:
                step.loop(i, 2 * 4)
                delta_units(i * 2 + 1, 1)
                delta_units(i * 2 + 2, 0)
                step.end(NH // 2 - 1)
            delta_units(NH - 1, 1)
            def dgate(i, s):
                act.wait_ge(unit_done[s], i + (B_GD // 2 + 1) + ONE)
                nc.scalar.activation(row_k(R2, i * 2 + s), bank[s][:, :], ACT.Tanh, scale=0.5
                                     ).then_inc(bank_free[s], 1)

            for j in range(4):
                delta_part(NH - 1, 1, j)
                if j == 0:
                    act.wait_ge(d_done, NH - 1 + ONE)
                if j == 3:
                    root_out(NH - 1)
                ahead_of_unit(NH - 1, j)
                dgate(j // 2, j % 2)
            act.wait_ge(d_done, NH + ONE)
            with act.Fori(2, U_GD // 2) as i:
                for s in range(2):
                    dgate(i, s)
            act.wait_ge(unit_done[1], B_WDO // 2 + ONE)
            for k in range(KT):
                nc.scalar.activation(xh[:, k, :], R1[:, k, :], ACT.Copy).then_inc(s_oh, 1)
            act.wait_ge(s_ol, KT)
            act.dma_start(R1[:, :, :], ga_d).then_inc(s_gal, 16)
            act.wait_ge(unit_done[1], B_MIX // 2 + ONE)
            for k in range(KT):
                act.wait_ge(s_mrg, k + 1)
                nc.scalar.activation(xh[:, k, :], R1[:, k, :], ACT.Copy, scale=0.5).then_inc(s_mh, 1)
            act.wait_ge(s_ml, KT)
            act.dma_start(R1[:, :, :], xT.rearrange("(k p) t -> p k t", p=P)).then_inc(s_xr, 16)
            for k in range(KT):
                act.wait_ge(bank_free[k % 2], B_MIX // 2 + k // 2 + 1)
                act.wait_ge(s_ss, KT + k - 1)
                nc.scalar.activation(sq[k % 2][:, :], R2[:, k, :], ACT.Square).then_inc(s_sq, 1)
            inverse_root(1)
            for k in range(KT):
                act.wait_ge(s_x2, k + 1)
                act.wait_ge(s_ss, 2 * KT + k - 1)
                nc.scalar.activation(sq[k % 2][:, :], R1[:, k, :], ACT.Square).then_inc(s_sq, 1)
            act.dma_start(x2_d, R1[:, :, :]).then_inc(s_x2d, 16)
            inverse_root(2)
            act.wait_ge(unit_done[1], B_Q // 2 + ONE)
            for k in range(KT):
                act.wait_ge(s_h, KT + k + 1)
                shifted(k, xh, R2, part(SHIFT_F), s_hi)
            act.wait_ge(s_x2d, 16)

            act.wait_ge(s_h, 2 * KT)
            act.dma_start(skz_sb[:, :, :], skz).then_inc(q_sk, 16)
            def early(b, done, chunk, count, tile=etile, slot=None):
                if slot is None:
                    act.wait_ge(unit_done[b], done + ONE)
                else:
                    act.wait_ge(unit_done[slot], HIGH_USES + ONE)
                act.wait_ge(e_st[b], count * 16 + DMA1)
                nc.scalar.activation(tile[b][:, :], bank[b][:, :], ACT.Gelu).then_inc(bank_free[b], 1)
                act.wait_ge(bank_free[b], done)
                act.dma_start(act_d[bass.ds(chunk, 1), :, :].rearrange("a p t -> (a p) t"), tile[b][:, :]
                              ).then_inc(e_st[b], 16)

            with act.Fori(0, PH // 2) as i:
                for s in range(2):
                    h = i * 2 + s
                    u = [i * 3 + (B_Q // 2 + (3 * s + n) // 2 + 1) for n in range(3)]
                    act.wait_ge(unit_done[s], u[0] + ONE)
                    nc.scalar.activation(qs[s][:, :], bank[s][:, :], ACT.Copy).then_inc(bank_free[s], 1)
                    act.wait_ge(q_sc, h + 1)
                    act.wait_ge(q_done, h + ONE)
                    for b in range(2):
                        ins = nc.scalar.activation(Sc[:, 2 * b:2 * b + 2, :].rearrange("p t n -> p (t n)"),
                                                   bank[2 + b][:, :], ACT.Copy)
                    ins.then_inc(q_s, 1)
                    early(1 - s, u[1], i * 4 + 2 * s, i * 2 + s)
                    act.wait_ge(q_nb, h + 1)
                    nc.scalar.activation(be[:, :, :], be[:, :, :], ACT.Exp).then_inc(q_e, 1)
                    early(s, u[2], i * 4 + (2 * s + 1), i * 2 + s)
            for j in range(U_TURN):
                if j == 2:
                    for n, dst in enumerate((i1T, i2T, gwT)):
                        act.wait_ge(g_tr, n + 1)
                        nc.scalar.activation(dst[:, :], bank[2 + n][:, :], ACT.Copy).then_inc(g_it, 1)
                early(j % 2, B_TURN // 2 + j // 2 + 1, 2 * PH + j, PH + j // 2)
            with act.Fori(0, T // 64) as i:
                for n in range(8):
                    st, sub = n // 4, n % 4
                    if sub == 0:
                        act.wait_ge(g_dma[st], i * 16 + DMA1)
                    act.wait_ge(g_mm, i * 8 + n + 1 + ONE)
                    for b in range(2):
                        t0 = sub * 8 + b * 4
                        ins = nc.scalar.activation(stage[st][:, :, t0:t0 + 4].rearrange("p i t -> p t i"),
                                                   bank4[2 + 2 * (n % 2) + b], ACT.Copy)
                    ins.then_inc(g_ev, 1)
                    if sub == 3:
                        act.wait_ge(g_ev, i * 8 + n + 1 + ONE)
                        act.dma_start(G_d[:, :, bass.ds(i * 64 + st * 32, 32)].rearrange("i j t -> j i t"),
                                      stage[st][:, :, :]).then_inc(g_dma[st], 16)
                    if n % 2:
                        j = n // 2
                        early(j % 2, i * 2 + (B_G // 2 + j // 2 + 1), i * 4 + (2 * PH + U_TURN + j),
                              i * 2 + (PH + U_TURN // 2 + j // 2))
            def load_weights(m):
                act.dma_start(Gt[:, :, :], G_d[bass.ds(m * 2, 2), :, :].rearrange("i j t -> j i t")
                              ).then_inc(p_g, 16)

            def upper_coefficients(m, par):
                for j in range(2):
                    act.wait_ge(p_cf, m * 2 + j + 1 + ONE)
                    nc.scalar.activation(CH[par][j][:, :], cf[j], ACT.Copy).then_inc(p_ch, 1)

            def gelus(m, slots, use, par):
                for j in range(2):
                    act.wait_ge(unit_done[slots[j]], use + ONE)
                    act.wait_ge(p_cl, m * 2 + ONE)
                    nc.scalar.activation(cf[j], bank[j][:, :], ACT.Gelu).then_inc(bank_free[j], 1)
                act.wait_ge(unit_done[1], m + (LOW_USES + EARLY_USES - EARLY) + ONE)
                upper_coefficients(m, par)

            def load_activations(m):
                act.wait_ge(p_cl, m * 2 + ONE)
                act.dma_start(cf2[:, :, :], act_d[bass.ds(m * 2, 2), :, :].rearrange("i j t -> j i t")
                              ).then_inc(p_act, 16)

            def late(n):
                early(n % 2, B_AFTER // 2 + n // 2 + 1, 2 * EARLY - U_AFTER + n, EARLY - U_AFTER // 2 + n // 2,
                      elate, slot=n if n >= 2 else None)

            late(0)
            for s in range(2):
                act.wait_ge(g_dma[s], T // 64 * 16 + DMA1)
            load_weights(0)
            load_activations(0)
            late(1)
            upper_coefficients(0, 0)
            act.wait_ge(p_cf, 2 + ONE)
            load_weights(1)
            load_activations(1)
            late(2)
            late(3)
            for b in range(2):
                act.wait_ge(e_st[b], EARLY * 16 + DMA1)
            upper_coefficients(1, 1)
            with act.Fori(1, EARLY // 2) as i:
                for e in range(2):
                    m = i * 2 + e
                    act.wait_ge(p_cf, m * 2 + ONE)
                    load_weights(m)
                    load_activations(m)
                    act.wait_ge(unit_done[1 + 2 * e], i + (HIGH_USES if e else LOW_USES) + ONE)
                    upper_coefficients(m, e)
            act.wait_ge(p_cf, EARLY * 2 + ONE)
            load_weights(EARLY)
            gelus(EARLY, (0, 1), LOW_USES + EARLY_USES + 1, 0)
            load_weights(EARLY + 1)
            with act.Fori(0, (PAIRS - EARLY) // 2 - 1) as i:
                for e in range(2):
                    gelus(i * 2 + (EARLY + e + 1), (2, 3), i * 2 + (HIGH_USES + EARLY_USES + e + 1), (e + 1) % 2)
                    load_weights(i * 2 + (EARLY + e + 2))
            gelus(PAIRS - 1, (2, 3), HIGH_USES + EARLY_USES + PAIRS - EARLY - 1, 1)
            act.dma_start(x2b[:, :, :], x2_d).then_inc(s_x2l, 16)
            for k in range(KT):
                act.wait_ge(p_add, (PAIRS - 1) * KT + k + 1 + ONE)
                act.wait_ge(s_ss, 3 * KT + k - 1)
                nc.scalar.activation(sq[k % 2][:, :], R1[:, k, :], ACT.Square).then_inc(s_sq, 1)
            inverse_root(3, bank[0])

        @block.vector
        def _(dve):
            step = Steps(dve, dve_step)
            v = nc.vector
            ahead = (d_done, d_sso, d_rso, q_done, q_s, g_mm, g_ev, p_add, p_cf, p_cl, s_adamm, *half_used,
                     *unit_done, *arow_used)
            for n, x in enumerate(ahead):
                v.memset(spare[:, n:n + 1], 0.0).then_inc(x, ONE)
            for n, x in enumerate(g_dma + e_st):
                v.memset(spare[:, 24 + n:25 + n], 0.0).then_inc(x, DMA1)
            v.memset(ones[:, :], 1.0)
            v.memset(eps[:, 0:1], EPS)
            v.memset(eps[:, 1:2], 1.0).then_inc(s_const, 1)
            dve.wait_ge(s_tanh, 1)
            step(v.scalar_tensor_tensor(cond[:, :], cond[:, :], 1.0, vec[:, V_C:V_C + KT], ALU.add, ALU.mult))
            step.sync()
            step(v.tensor_scalar(cond[:, :], cond[:, :], 0.5, None, ALU.mult))

            step.sync()
            with dve.Fori(0, 2) as c:
                for k in range(KT):
                    s = k % 4
                    dve.wait_ge(arow_full[s], (c * (KT // 4) + (k // 4 + 1)) * 16)
                    if k == 0:
                        dve.wait_ge(s_adamm, c + ONE)
                        v.tensor_scalar(acc[:, :], arow[0][:, :], cond[:, 0:1], None, ALU.mult
                                        ).then_inc(arow_used[0], 1)
                    else:
                        dve.wait_ge(arow_used[(k - 1) % 4], c * (KT // 4) + ((k - 1) // 4 + 1) + ONE)
                        v.scalar_tensor_tensor(acc[:, :], arow[s][:, :], cond[:, k:k + 1], acc[:, :],
                                               ALU.mult, ALU.add).then_inc(arow_used[s], 1)
                dve.wait_ge(s_adamm, c + 1 + ONE)
                v.tensor_tensor(ada[:, bass.ds(c * KT, KT)], bank[0][:, 0:KT], vec[:, bass.ds(c * KT + V_BADA, KT)],
                                ALU.add).then_inc(s_ada, 1)

            def gains(n, m):
                g = vec[:, V_NORM + n * KT:V_NORM + (n + 1) * KT]
                step(v.scalar_tensor_tensor(coef[:, n, :], part(m), 0.0 if n % 2 else 1.0, g, ALU.add, ALU.mult))

            dve.wait_ge(s_ada, 2)
            gains(0, SCALE_M)
            step.sync()

            def modulated(n, i, src, dst, shift):
                dve.wait_ge(s_rs, i + 1)
                for k in range(KT + 1):
                    if k < KT:
                        v.scalar_tensor_tensor(dst[:, k, :], src[:, k, :], coef[:, n, k:k + 1], rs[:, :],
                                               ALU.mult, ALU.mult).then_inc(s_h, 1)
                    if k:
                        dve.wait_ge(s_hi, n // 2 * KT + k)
                        v.scalar_tensor_tensor(xl[:, k - 1, :], dst[:, k - 1, :], shift[:, k - 1:k],
                                               xh[:, k - 1, :].bitcast(F32), ALU.add, ALU.subtract).then_inc(s_lo, 1)

            modulated(0, 0, R1, R1, part(SHIFT_M))

            def rows():
                dve.wait_ge(s_ba, 1)
                dve.wait_ge(s_rowa, 1)
                A = slice(32, 48)
                step(v.memset(row[1][:, :], 0.0))
                step.sync()
                step(v.tensor_scalar(row[1][0:16, :], row[0][0:16, :], 1.0, 0.5, ALU.add, ALU.mult))
                step(v.tensor_scalar(row[1][A, :], bank[2][A, :], vec[A, V_AD + 1:V_AD + 2], None, ALU.add))
                step.sync()
                v.scalar_tensor_tensor(row[2][A, :], row[1][A, :], -1.0, row[1][A, :], ALU.mult, ALU.max
                                       ).then_inc(s_rowb, 1)
                dve.wait_ge(s_rowa, 2)
                step(v.scalar_tensor_tensor(row[2][A, :], row[1][A, :], 0.0, row[2][A, :], ALU.max, ALU.add))
                step.sync()
                step(v.tensor_scalar(row[2][A, :], row[2][A, :], row[3][A, 1:2], None, ALU.mult))
                step.sync()
                for c in range(4):
                    ins = v.tensor_tensor_scan(cc(row[1][A, :], c), cc(row[2][A, :], c), cc(row[2][A, :], c), 0.0,
                                               ALU.add, ALU.bypass)
                ins.then_inc(s_row, 1)

            def rotate(h, a):
                n, u = h * 6 + (a // 3) * 2 + a % 3, h * 9 + a
                x = qk[h % 2][(a // 3) * 2 + a % 3][0:32, :]
                dve.wait_ge(bank_free[u % 2], u // 2 + 1)
                dve.wait_ge(s_rot, n + 1)
                step(v.tensor_tensor(rtmp[:, :], bank[2][0:32, :], acst[0:32, K_SIN:K_SIN + T], ALU.mult))
                step(v.tensor_tensor(x, x, acst[0:32, K_COS:K_COS + T], ALU.mult))
                step.sync()
                v.tensor_tensor(x, x, rtmp[:, :], ALU.add).then_inc(s_rotd, 1)

            def mask_scores(h, i):
                t = h * 4 + i
                n0, n1 = (1 if i == 0 else 2) * P, (i + 1) * P
                dve.wait_ge(s_S, t + 1)
                if t:
                    dve.wait_ge(s_tr, t)
                step(v.scalar_tensor_tensor(prob[:, 0:n0], bank[4][:, 0:n0], SCALE,
                                            acst[:, K_MASK + 2 * P - n0:K_MASK + 2 * P], ALU.mult, ALU.add))
                for g in (1, 2):
                    end = K_MASK + (2 + 4 * g) * P
                    step(v.scalar_tensor_tensor(prob[:, n0 + (g - 1) * n1:n0 + g * n1], bank[4 + g][:, 0:n1], SCALE,
                                                acst[:, end - n1:end], ALU.mult, ALU.add))
                step.sync()
                step(v.tensor_reduce(mcol[:, 2:3], prob[:, 0:n0 + 2 * n1], AX.X, ALU.max))
                step.sync()
                v.tensor_scalar(mcol[:, 0:1], mcol[:, 2:3], -1.0, None, ALU.mult).then_inc(s_nm, 1)
                dve.wait_ge(s_exp, t + 1)
                step(v.reciprocal(mcol[:, 3:4], mcol[:, 1:2]))
                step.sync()
                v.tensor_scalar(prob[:, 0:n0 + 2 * n1], prob[:, 0:n0 + 2 * n1], mcol[:, 3:4], None, ALU.mult
                                ).then_inc(s_P, 1)

            def late_halves(n0):
                for n in range(n0, min(n0 + 2, HALVES)):
                    q, k, s = n // KT, n % KT, n % 2
                    dve.wait_ge(half_full[s], (n // 2 + 1) * 16)
                    if k == 0:
                        v.tensor_scalar(hacc[q % 2][:, :], half[s][:, :], cond[:, 0:1], None, ALU.mult
                                        ).then_inc(half_used[s], 1)
                    else:
                        dve.wait_ge(half_used[1 - s], (n - 1) // 2 + 1 + ONE)
                        v.scalar_tensor_tensor(hacc[q % 2][:, :], half[s][:, :], cond[:, k:k + 1],
                                               hacc[q % 2][:, :], ALU.mult, ALU.add).then_inc(half_used[s], 1)

            for h in range(AH):
                for a in range(9):
                    u = h * 9 + a
                    late_halves(4 * u)
                    if u in sums_at:
                        q = sums_at.index(u)
                        c = slice((4 + q) * KT // 2, (5 + q) * KT // 2)
                        dve.wait_ge(s_adamm, 3 + q + ONE)
                        v.tensor_tensor(ada[:, c], bank[3][:, 0:KT // 2], vec[:, c], ALU.add).then_inc(s_ada, 1)
                    if u == 1:
                        rows()
                    if u == 2:
                        dve.wait_ge(s_turn, 1)
                        v.tensor_copy(bycol[:, :, :], bank4[3][:, :, 0:48]).then_inc(s_bycol, 1)
                    if h >= 1 and a < 8 and a % 2 == 0:
                        mask_scores(h - 1, a // 2)
                    if a >= 1 and (a - 1) % 3 < 2:
                        rotate(h, a - 1)
                    late_halves(4 * u + 2)
            dve.wait_ge(s_ada, 2 + HALVES // KT)
            for n, m in ((1, GATE_M), (2, SCALE_F), (3, GATE_F)):
                gains(n, m)
            for i in range(4):
                mask_scores(AH - 1, i)

            dve.wait_ge(s_yh, 1)
            v.tensor_tensor(yl[:, :, :], YA[:, :, :], yh[:, :, :].bitcast(F32), ALU.subtract).then_inc(s_yl, 1)
            for b in range(2):
                dve.wait_ge(bank_free[b], B_WAO // 2)
            for w in range(U_WAO):
                u = B_WAO + w
                for n in range(4):
                    if n < 3:
                        dve.wait_ge(s_wao, 3 * w + n + 1)
                    else:
                        dve.wait_ge(unit_done[u % 2], u // 2 + 1 + ONE)
                    x = R2[:, 4 * w + n, :]
                    v.scalar_tensor_tensor(x, x, 1.0, bank[2 + n][:, :], ALU.add, ALU.mult
                                           ).then_inc(s_waoc if n < 3 else bank_free[u % 2], 1)

            def b4(x):
                return x.unsqueeze(1).to_broadcast([P, 4, P])

            def r4(x):
                return x[:, :].rearrange("p (c n) -> p c n", c=4)

            def level(lv):
                return b4(cst[:, C_LEV + lv * P:C_LEV + (lv + 1) * P])

            def all_packed(b, lv):
                return b[:, 0:T // 2].rearrange("p (b s) -> p b s", s=2 << lv)

            def next_level(h, lv):
                if lv < LEVELS - 2:
                    v.tensor_tensor(r4(bt[lv % 2]), r4(LT), level(lv + 2), ALU.mult).then_inc(d_bt, 1)
                dve.wait_ge(d_xx, h * (LEVELS - 1) + lv + 1)
                dve.wait_ge(d_x, h * LEVELS + lv + 1)
                if lv < LEVELS - 2:
                    x = half_columns(X[:, :], lv, 0)
                    v.tensor_tensor(x, x, all_packed(bank[5], lv), ALU.subtract)
                x = half_columns(XT[:, :], lv, 1)
                v.tensor_tensor(x, x, all_packed(bank[6], lv), ALU.subtract).then_inc(d_x, 1)

            def ahead_of_unit(h, j):
                if j < 2:
                    next_level(h, 3 * j)
                if j == 2:
                    dve.wait_ge(d_st, h * 3 + 1)
                    v.tensor_copy(st_s[:, :], bank[5][:, 0:P]).then_inc(d_s, 1)

            def delta_part(h, p, j):
                if j == 0:
                    for x, n in ((bcol, 0), (gcol, 32)):
                        step(v.tensor_copy(x[:, :], bycol[:, :, h + n] if isinstance(h, int) else
                                           bycol[:, :, bass.ds(h + n, 1)].rearrange("p c a -> p (c a)")))
                    dve.wait_ge(d_bc, (h + 1) * 32)
                    step.sync()
                    for c in range(4):
                        ins = v.scalar_tensor_tensor(cc(dec, c), cc(BG, c), gcol[:, c:c + 1],
                                                     cst[:, C_NEG:C_NEG + P], ALU.subtract, ALU.add)
                    ins.then_inc(d_dd, 1)
                    v.tensor_tensor(kcol[:, :], BG[:, P - 1::P], gcol[:, :], ALU.subtract).then_inc(d_kc, 1)
                    dve.wait_ge(d_egc, h + 1)
                    step(v.scalar_tensor_tensor(nbeg[:, :], bcol[:, :], -1.0, egc[:, :], ALU.mult, ALU.mult))
                    dve.wait_ge(d_dec, h + 1)
                    step(v.tensor_tensor(bt[0][:, :], dec[:, :], BB[:, :], ALU.mult))
                    dve.wait_ge(d_p1, h * 4 + 2)
                    step.sync()
                    step(v.tensor_tensor(LT[:, :], bank[4][:, :], bt[0][:, :], ALU.mult))
                    step(v.tensor_tensor(qks[:, :], bank[3][:, :], dec[:, :], ALU.mult))
                    step.sync()
                    v.tensor_tensor(r4(bt[0]), r4(LT), level(0), ALU.mult).then_inc(d_b0, 1)
                    dve.wait_ge(d_b0, h + 1)
                    step(v.tensor_tensor(r4(XT), b4(ident), r4(bt[0]), ALU.subtract))
                    v.tensor_tensor(r4(bt[1]), r4(LT), level(1), ALU.mult).then_inc(d_bt, 1)
                    dve.wait_ge(d_eg, h + 1)
                    v.tensor_tensor(qd[:, :], dq[p][:, :], eg[:, :], ALU.mult).then_inc(d_in, 1)
                    dve.wait_ge(d_b0t, h + 1)
                    step.sync()
                    v.tensor_tensor(r4(X), b4(ident), bank4[3], ALU.subtract).then_inc(d_x, 1)
                if j in (1, 2):
                    for lv in range(3 * j - 2, 3 * j):
                        next_level(h, lv)
                if j == 3:
                    for c in range(1, 4):
                        dve.wait_ge(d_ks, h * 3 + c)
                        v.scalar_tensor_tensor(st_r[:, :], bank[3][:, 0:P], nbeg[:, c:c + 1], cc(vb, c),
                                               ALU.mult, ALU.add).then_inc(d_r, 1)
                        if c < 3:
                            dve.wait_ge(d_st, h * 3 + c + 1)
                            dve.wait_ge(d_s, h * 3 + c)
                            v.scalar_tensor_tensor(st_s[:, :], st_s[:, :], eg[:, (c + 1) * P - 1:(c + 1) * P],
                                                   bank[5][:, 0:P], ALU.mult, ALU.add).then_inc(d_s, 1)

            def output(h, p):
                dve.wait_ge(d_rso, h + 1 + ONE)
                step(v.tensor_tensor(T1[:, :], bank[7][:, :], drs[:, :], ALU.mult))
                step.sync()
                v.scalar_tensor_tensor(row_k(R1, h), T1[:, :], dnw[:, 0:1], dz[p][:, :], ALU.mult, ALU.mult
                                       ).then_inc(d_done, 1)

            def delta_units(h, p):
                first = isinstance(h, int) and h == 0
                for j in range(4):
                    if not first:
                        delta_part(h - 1, 1 - p, j)
                    if j in (1, 2):
                        x = (dq, dk)[j - 1][p]
                        dve.wait_ge(d_rse, h * 2 + j)
                        if j == 1:
                            v.scalar_tensor_tensor(x[:, :], x[:, :], SCALE, drs[:, :], ALU.mult, ALU.mult
                                                   ).then_inc(d_nrm, 1)
                        else:
                            v.tensor_tensor(x[:, :], x[:, :], drs[:, :], ALU.mult).then_inc(d_nrm, 1)
                    use = h * 2 + (B_DN // 2 + j // 2 + 1)
                    if j == 0:
                        src = vec[:, V_CONV:V_CONV + 12] if first else vec[:, bass.ds(h * 12 + V_CONV, 12)]
                        step(v.tensor_scalar(cw[:, :], src, 0.5, None, ALU.mult))
                    if j < 3:
                        dve.wait_ge(unit_done[j % 2], use + ONE)
                        step.sync()
                        y = bank[j % 2]
                        step(v.tensor_scalar(cv[:, :], y[:, :], cw[:, 4 * j + 3:4 * j + 4], None, ALU.mult))
                        for n in (1, 2, 3):
                            step.sync()
                            ins = v.scalar_tensor_tensor(cv[:, n:], y[:, 0:T - n], cw[:, 4 * j + 3 - n:4 * j + 4 - n],
                                                         cv[:, n:], ALU.mult, ALU.add)
                            if n < 3:
                                step(ins)
                        ins.then_inc(bank_free[j % 2], 1)
                        if not first:
                            ahead_of_unit(h - 1, j)
                        dve.wait_ge(bank_free[j % 2], use)
                        dve.wait_ge(d_th, h * 4 + j + 1)
                        v.scalar_tensor_tensor((dq, dk, dv)[j][p][:, :], th[:, :], 1.0, cv[:, :], ALU.add, ALU.mult
                                               ).then_inc(d_e, 1)
                    else:
                        dve.wait_ge(d_th, h * 4 + j + 1)
                        v.scalar_tensor_tensor(dz[p][:, :], th[:, :], 1.0, bank[1][:, :], ALU.add, ALU.mult
                                               ).then_inc(bank_free[1], 1)
                        if not first:
                            dve.wait_ge(bank_free[1], use)
                            output(h - 1, 1 - p)

            dve.wait_ge(s_gad, 16)
            v.tensor_scalar(dnw[:, :], vec[:, V_DNW:V_DNW + 1], 0.5, None, ALU.mult)
            delta_units(0, 0)
            with dve.Fori(0, NH // 2 - 1) as i:
                step.loop(i, 2 * 18)
                delta_units(i * 2 + 1, 1)
                delta_units(i * 2 + 2, 0)
                step.end(NH // 2 - 1)
            delta_units(NH - 1, 1)
            for j in range(4):
                delta_part(NH - 1, 1, j)
                ahead_of_unit(NH - 1, j)
            output(NH - 1, 1)

            for k in range(KT):
                dve.wait_ge(s_oh, k + 1)
                v.tensor_tensor(xl[:, k, :], R1[:, k, :], xh[:, k, :].bitcast(F32), ALU.subtract).then_inc(s_ol, 1)
            dve.wait_ge(s_gal, 16)
            with dve.Fori(0, U_WDO // 2) as i:
                for s in range(2):
                    dve.wait_ge(unit_done[s], i + (B_WDO // 2 + 1) + ONE)
                    x, g = row_k(R1, i * 2 + s), row_k(R2, i * 2 + s)
                    v.scalar_tensor_tensor(g, g, 1.0, bank[s][:, :], ALU.add, ALU.mult).then_inc(bank_free[s], 1)
                    dve.wait_ge(bank_free[s], i + (B_WDO // 2 + 1))
                    v.tensor_tensor(x, x, g, ALU.add).then_inc(s_mrg, 1)
            for k in range(KT):
                dve.wait_ge(s_mh, k + 1)
                v.scalar_tensor_tensor(xl[:, k, :], R1[:, k, :], 0.5, xh[:, k, :].bitcast(F32), ALU.mult,
                                       ALU.subtract).then_inc(s_ml, 1)
            def add_square(n, k):
                dve.wait_ge(s_sq, n * KT + k + 1)
                if k:
                    dve.wait_ge(s_ss, n * KT + k)
                    v.tensor_tensor(ssum[:, :], ssum[:, :], sq[k % 2][:, :], ALU.add).then_inc(s_ss, 1)
                else:
                    v.tensor_copy(ssum[:, :], sq[0][:, :]).then_inc(s_ss, 1)

            for k in range(KT + 1):
                if k < KT:
                    dve.wait_ge(unit_done[k % 2], B_MIX // 2 + k // 2 + 1 + ONE)
                    v.tensor_copy(R2[:, k, :], bank[k % 2][:, :]).then_inc(bank_free[k % 2], 1)
                if k:
                    add_square(1, k - 1)
            dve.wait_ge(s_rs, 2)
            dve.wait_ge(s_xr, 16)
            for b in range(2):
                dve.wait_ge(bank_free[b], B_Q // 2)
            for k in range(KT):
                step(v.scalar_tensor_tensor(R2[:, k, :], R2[:, k, :], coef[:, 1, k:k + 1], rs[:, :],
                                            ALU.mult, ALU.mult))
                step.sync()
                v.tensor_tensor(R1[:, k, :], R1[:, k, :], R2[:, k, :], ALU.add).then_inc(s_x2, 1)
            modulated(2, 2, R1, R2, part(SHIFT_F))

            def settle():
                step.sync()
                v.memset(scrap[:, :], 0.0)

            def best16(out, idx, src, rest):
                settle()
                for o, x in zip(out, src):
                    step(v.max(o[:, 0:8], x))
                settle()
                for o, n, x, y in zip(out, idx, src, rest):
                    step(v.max_index(n[:, 0:8], o[:, 0:8], x))
                    step(v.match_replace(y, o[:, 0:8], x, LOW))
                settle()
                for o, y in zip(out, rest):
                    step(v.max(o[:, 8:16], y))
                settle()
                for o, n, y in zip(out, idx, rest):
                    step(v.max_index(n[:, 8:16], o[:, 8:16], y))
                settle()

            def choose(h):
                dve.wait_ge(q_s, h + 1 + ONE)
                sets = [(t, half) for t in range(TT) for half in range(2)]
                best16([hs[:, t, a, :] for t, a in sets], [hiu[:, t, a, :] for t, a in sets],
                       [Sc[:, t, a * P:(a + 1) * P] for t, a in sets], [Sc2[:, t, a * P:(a + 1) * P] for t, a in sets])
                step(v.tensor_copy(hif[:, :, :, :], hiu[:, :, :, :]))
                for t in range(TT):
                    step(v.tensor_tensor(cand[:, t, :].rearrange("p (a b) -> p a b", a=TOPK),
                                         hs[:, t, 0, :].unsqueeze(2).to_broadcast([P, TOPK, TOPK]),
                                         hs[:, t, 1, :].unsqueeze(1).to_broadcast([P, TOPK, TOPK]), ALU.add))
                best16([bs[:, t, :] for t in range(TT)], [bp[:, t, :] for t in range(TT)],
                       [cand[:, t, :] for t in range(TT)], [cand2[:, t, :] for t in range(TT)])
                v.tensor_tensor(be[:, :, :], bs[:, :, :], bs[:, :, 0:1].to_broadcast([P, TT, TOPK]), ALU.subtract
                                ).then_inc(q_nb, 1)
                step(v.tensor_scalar(pu[:, 0, :], bp[:, :, :].rearrange("p t k -> p (t k)"), 4, None,
                                     ALU.logical_shift_right))
                step(v.tensor_scalar(pu[:, 1, :], bp[:, :, :].rearrange("p t k -> p (t k)"), 15, None,
                                     ALU.bitwise_and))
                step.sync()
                step(v.tensor_copy(pf[:, :, :], pu[:, :, :]))
                step.sync()
                for half, dst in ((0, I1), (1, I2)):
                    n = TT * TOPK
                    step(v.tensor_tensor(pick[:, :, :], pf[:, half, :].unsqueeze(2).to_broadcast([P, n, TOPK]),
                                         iota[:, 0:TOPK].unsqueeze(1).to_broadcast([P, n, TOPK]), ALU.is_equal))
                    step.sync()
                    p4 = pick[:, :, :].rearrange("p (t k) a -> p t k a", t=TT)
                    step(v.tensor_tensor(p4, p4, hif[:, :, half, :].unsqueeze(2).to_broadcast([P, TT, TOPK, TOPK]),
                                         ALU.mult))
                    step.sync()
                    step(v.tensor_reduce(pr[:, :], pick[:, :, :], AX.X, ALU.add))
                    step.sync()
                    step(v.tensor_copy(dst[:, :, bass.ds(h * TOPK, TOPK)],
                                       pr[:, :].rearrange("p (t k) -> p t k", t=TT)))
                dve.wait_ge(q_e, h + 1)
                step(v.tensor_reduce(bsum[:, 0:TT], be[:, :, :], AX.X, ALU.add))
                step.sync()
                step(v.reciprocal(bsum[:, TT:2 * TT], bsum[:, 0:TT]))
                step.sync()
                v.tensor_tensor(GW[:, :, bass.ds(h * TOPK, TOPK)], be[:, :, :],
                                bsum[:, TT:2 * TT].unsqueeze(2).to_broadcast([P, TT, TOPK]), ALU.mult
                                ).then_inc(q_done, 1)

            with dve.Fori(0, PH) as h:
                step.loop(h, 78)
                choose(h)
                step.end(PH)

            dve.wait_ge(g_it, 3)
            with dve.Fori(0, T // 64) as i:
                for n in range(8):
                    dve.wait_ge(g_mm, i * 8 + max(n - 1, 0) + ONE)
                    for j in range(8):
                        t = bass.ds(i * 64 + (n * 8 + j), 1)
                        v.tensor_scalar(hotA[n % 2][:, j, :], iota, i1T[:, t], gwT[:, t], ALU.is_equal, ALU.mult)
                        ins = v.tensor_scalar(hotB[n % 2][:, j, :], iota, i2T[:, t], None, ALU.is_equal)
                    ins.then_inc(g_ab, 1)

            for s in range(2):
                dve.wait_ge(g_dma[s], T // 64 * 16 + DMA1)

            def coefficients(m, par, early=False):
                dve.wait_ge(p_g, m * 16 + 16)
                for j in range(2):
                    if early:
                        dve.wait_ge(p_act, m * 16 + 16)
                    else:
                        dve.wait_ge(bank_free[j], m + (SLOT_USES - EARLY + 1))
                    v.tensor_tensor(cf[j], cf[j], Gt[:, j, :], ALU.mult).then_inc(p_cf, 1)
                for j in range(2):
                    dve.wait_ge(p_ch, m * 2 + j + 1)
                    v.tensor_tensor(CL[par][j][:, :], cf[j], CH[par][j][:, :].bitcast(F32), ALU.subtract
                                    ).then_inc(p_cl, 1)

            def accumulate(m, slot, use, first=False):
                for n in range(KT):
                    if n < KT - 1:
                        dve.wait_ge(p_y, m * (KT - 1) + n + 1)
                    else:
                        dve.wait_ge(unit_done[slot], use + ONE)
                    dve.wait_ge(p_add, m * KT + ONE)
                    y = bank[2 + n % 6][:, :]
                    if first:
                        ins = v.tensor_copy(R1[:, n, :], y)
                    else:
                        ins = v.tensor_tensor(R1[:, n, :], R1[:, n, :], y, ALU.add)
                    ins.then_inc(p_add, 1)

            def two_pairs(i, first=False):
                coefficients(i * 2 + 1, 1, True)
                accumulate(i * 2, 1, i + (LOW_USES + 1), first)
                coefficients(i * 2 + 2, 0, True)
                accumulate(i * 2 + 1, 3, i + (HIGH_USES + 1))

            coefficients(0, 0, True)
            two_pairs(0, True)
            with dve.Fori(1, EARLY // 2 - 1) as i:
                two_pairs(i)
            coefficients(EARLY - 1, 1, True)
            accumulate(EARLY - 2, 1, EARLY_USES + LOW_USES)
            accumulate(EARLY - 1, 3, EARLY_USES + HIGH_USES)
            coefficients(EARLY, 0)
            with dve.Fori(0, (PAIRS - EARLY) // 2 - 1) as i:
                for e in range(2):
                    coefficients(i * 2 + (EARLY + e + 1), (e + 1) % 2)
                    accumulate(i * 2 + (EARLY + e), 1, i * 2 + (e + LOW_USES + EARLY_USES + 2))
            coefficients(PAIRS - 1, 1)
            accumulate(PAIRS - 2, 1, PAIRS - EARLY + LOW_USES + EARLY_USES)
            accumulate(PAIRS - 1, 3, PAIRS - EARLY + HIGH_USES + EARLY_USES)
            dve.wait_ge(p_add, PAIRS * KT + ONE)
            dve.wait_ge(s_rs, 4)
            dve.wait_ge(s_x2l, 16)
            for k in range(KT):
                step(v.scalar_tensor_tensor(R1[:, k, :], R1[:, k, :], coef[:, 3, k:k + 1], rs[:, :],
                                            ALU.mult, ALU.mult))
                step.sync()
                v.tensor_tensor(R1[:, k, :], R1[:, k, :], x2b[:, k, :], ALU.add).then_inc(s_out, 1)


def tables():
    j, i = np.arange(P)[:, None], np.arange(P)[None, :]
    c = np.zeros((P, C_N), np.float32)
    c[:, C_ID:C_ID + P] = j == i
    c[:, C_NEG:C_NEG + P] = np.where(i >= j, 0.0, -1e30)
    for lv in range(LEVELS):
        c[:, C_LEV + lv * P:C_LEV + (lv + 1) * P] = (i >> lv + 1 == j >> lv + 1) & (i >> lv & 1 == 1) & (j >> lv & 1 == 0)
    c[:, C_IOTA:C_IOTA + P] = i
    a = np.zeros((P, K_N), np.float32)
    q, k = j, i
    ok = [k >= q, k <= q]
    for dil in (4, 16):
        same = (q - k) % dil == 0
        ok += [same] * 3 + [same & (k <= q)]
    for n, m in enumerate(ok):
        a[:, K_MASK + n * P:K_MASK + (n + 1) * P] = np.where(m, 0.0, -1e30)
    half = P // 8
    inv = np.float32(500000.0) ** (-np.arange(half, dtype=np.float32) * np.float32(2.0 / (2 * half)))
    ang = np.arange(T, dtype=np.float32)[None, :] * inv.astype(np.float32)[:, None]
    a[0:2 * half, K_COS:K_COS + T] = np.cos(np.concatenate([ang, ang]))
    a[0:2 * half, K_SIN:K_SIN + T] = np.concatenate([-np.sin(ang), np.sin(ang)])
    for m in range(32):
        a[(m + 16) % 32, K_PERM + m] = 1.0
    return c, a


def units(w):
    k, n = w.shape
    return w.reshape(k // P, P, n // P, P).transpose(2, 1, 0, 3).reshape(n // P, P, -1)


def layout(x, c, w_ada, b_ada, norm_pre_mix, norm_post_mix, norm_pre_ffn, norm_post_ffn, w_in, conv_w, a_log,
           dt_bias, dn_norm_w, w_attn_out, w_delta_out, w_mix_out, peer_w_query, peer_sub_keys, peer_down, peer_up):
    w_in = w_in[0]
    W = AH * AG * P
    dn0 = 3 * W
    z0, b0 = dn0 + 3 * NH * P, dn0 + 4 * NH * P
    a0, g0 = b0 + NH, b0 + 2 * NH
    main = units(np.concatenate([w_in[:, :b0], w_in[:, g0:]], axis=1))
    att = [main[j * AH * AG + g * AH + h] for h in range(AH) for g in range(AG) for j in range(3)]
    first = 3 * AH * AG
    delta = [main[first + j * NH + h] for h in range(NH) for j in range(4)]
    gates = main[first + 4 * NH:]
    wao = units(w_attn_out[0]).reshape(U_WAO, 4, P, AH * P).transpose(0, 2, 1, 3).reshape(U_WAO, P, D)
    down = units(peer_down[0].T)
    up = peer_up[0].reshape(NCHUNK, P, D)
    query = units(peer_w_query[0])
    behind = []
    for h in range(PH):
        behind += [query[h:h + 1], down[2 * h:2 * h + 2]]
    behind += [down[2 * PH:2 * EARLY], up[:2 * EARLY], down[2 * EARLY:2 * EARLY + 2]]
    for m in range(EARLY, PAIRS - 1):
        behind += [down[2 * m + 2:2 * m + 4], up[2 * m:2 * m + 2]]
    behind += [up[-2:]]
    ada = w_ada[0].reshape(KT, P, 6, D).transpose(2, 0, 1, 3)
    stream = np.concatenate([
        ada[:2].reshape(U_ADA, P, D), np.stack(att), gates[:KT], wao,
        np.stack(delta), gates[KT:], units(w_delta_out[0]), units(w_mix_out[0])] + behind)
    vec = np.zeros((P, V_N), np.float32)

    def cols(w):
        return w.reshape(-1, P).T

    vec[:, V_BADA:V_NORM] = cols(b_ada[0])
    for n, w in enumerate((norm_pre_mix, norm_post_mix, norm_pre_ffn, norm_post_ffn)):
        vec[:, V_NORM + n * KT:V_NORM + (n + 1) * KT] = cols(w[0])
    vec[:, V_CONV:V_C] = conv_w[0].reshape(4, 3, NH, P).transpose(3, 2, 1, 0).reshape(P, NH * 12)
    vec[:, V_C:V_DNW] = cols(c[0])
    vec[:, V_DNW] = dn_norm_w[0]
    vec[32:48, V_AD] = a_log[0]
    vec[32:48, V_AD + 1] = dt_bias[0]
    wba = np.zeros((P, KT, 48), np.float32)
    wba[:, :, 0:16] = w_in[:, b0:a0].reshape(KT, P, NH).transpose(1, 0, 2)
    wba[:, :, 32:48] = w_in[:, a0:g0].reshape(KT, P, NH).transpose(1, 0, 2)
    skz = np.zeros((P, PH, 2, P), np.float32)
    for half in range(2):
        skz[64 * half:64 * half + 64, :, half, :] = peer_sub_keys[0][:, half].transpose(2, 0, 1)
    consts, aconsts = tables()
    late = ada[2:].reshape(4, KT, P, 2, D // 2).transpose(0, 3, 1, 2, 4).reshape(HALVES, P, D // 2)
    return {"stream": stream, "ada_late": np.ascontiguousarray(late), "xT": np.ascontiguousarray(x[0].T), "vecs": vec, "consts": consts,
            "aconsts": aconsts, "wba": wba, "skz": skz.reshape(P, PH, 2 * P)}


def kernel(**inputs):
    import concourse.bacc as _bacc
    from concourse.bass_utils import run_bass_kernel_spmd as _run

    arrays = layout(**{k: np.asarray(v) for k, v in inputs.items()})
    nc = _bacc.Bacc("TRN2", target_bir_lowering=False, num_devices=1)
    args = {n: nc.dram_tensor(n, a.shape, F32, kind="ExternalInput").ap() for n, a in arrays.items()}
    for name, shape in (("gam_d", [2 * NH, T]), ("ga_d", [P, KT, T]), ("x2_d", [P, KT, T]), ("G_d", [NCHUNK, P, T]),
                        ("act_d", [2 * EARLY, P, T])):
        args[name] = nc.dram_tensor(name, shape, F32).ap()
    out = nc.dram_tensor("outT", [D, T], F32, kind="ExternalOutput").ap()
    hybrid_block(nc, outT=out, **args)
    r = _run(nc, [arrays], core_ids=[0])
    return np.ascontiguousarray(r.results[0]["outT"].T)[None]
```
